# Optimizing a Trainium2 kernel written in Bass

```python
import math
import jax, jax.numpy as jnp
from jax import lax
import numpy as np

'''Hybrid chunk-causal streaming-encoder trunk (DEPTH layers).

Per layer:  x += 1/2 SwiGLU(RMSNorm(x));  x += MixerBlock(RMSNorm(x));  x += 1/2 SwiGLU(RMSNorm(x)).
MixerBlock: one combined input projection -> three parallel token mixers
  A: forgetting attention (FoX), B: Mamba-2 SSD, C: Griffin RG-LRU,
each projected to D_MODEL and merged by per-channel sigmoid gates computed from the
normalised input, then one output projection. 16 learned meta tokens are prepended
before layer 0 and dropped at the end; a final RMSNorm is applied.
Inputs: x (BATCH, SEQ, D_MODEL) float32 plus per-layer stacked parameters.
Output: (BATCH, SEQ, D_MODEL).
'''

D_MODEL = 1024
BATCH = 1
SEQ = 256
DEPTH = 1

CHUNK = 64
N_META = 16
Q_BLOCK = 2 * CHUNK
SSD_CHUNK = 2 * CHUNK
NORM_EPS = 1e-6

ATTN_HEADS = 16
ATTN_HEAD_DIM = 64
D_ATTN = ATTN_HEADS * ATTN_HEAD_DIM
FORGET_BIAS_INIT = 3.0

SSD_HEAD_DIM = 64
D_SSD = D_MODEL
SSD_HEADS = D_SSD // SSD_HEAD_DIM
SSD_GROUPS = 2
SSD_STATE = 128
SSD_CONV = 4
D_XBC = D_SSD + 2 * SSD_GROUPS * SSD_STATE

D_LRU = D_MODEL
LRU_BLOCKS = 16
LRU_BLOCK_DIM = D_LRU // LRU_BLOCKS
LRU_CONV = 4
LRU_C = 8.0

D_FF = 2816

N_BRANCH = 3
IN_SIZES = (D_ATTN, D_ATTN, D_ATTN, ATTN_HEADS, D_SSD, D_XBC, SSD_HEADS, D_LRU, D_LRU, N_BRANCH * D_MODEL)
N_IN = 3 * D_ATTN + ATTN_HEADS + D_SSD + D_XBC + SSD_HEADS + 2 * D_LRU + N_BRANCH * D_MODEL

kernel_name = 'hybrid_fox_ssd_rglru_macaron'

def _in_split_points():
    return [int(v) for v in np.cumsum(IN_SIZES)[:-1]]

def rms_norm(x, g):
    xf = x.astype(jnp.float32)
    y = xf * lax.rsqrt(jnp.mean(xf * xf, axis=-1, keepdims=True) + NORM_EPS)
    return (y * g.astype(jnp.float32)).astype(x.dtype)

def swiglu_ffn(h, w_gate_up, w_down):
    g, u = jnp.split(h @ w_gate_up, 2, axis=-1)
    return (jax.nn.silu(g) * u) @ w_down

def causal_depthwise_conv(x, w, b):
    k_width, c = w.shape
    y = lax.conv_general_dilated(x, w[:, None, :].astype(x.dtype), window_strides=(1,),
                                 padding=[(k_width - 1, 0)],
                                 dimension_numbers=('NWC', 'WIO', 'NWC'),
                                 feature_group_count=c)
    return y + b.astype(y.dtype)

def forgetting_attention(q, k, v, log_f):
    b, L, h, dh = q.shape
    c = jnp.cumsum(log_f, axis=1).transpose(0, 2, 1)
    scale = dh ** -0.5
    outs = []
    for start in range(0, L, Q_BLOCK):
        end = start + Q_BLOCK
        s = jnp.einsum('bqhd,bkhd->bhqk', q[:, start:end], k[:, :end],
                       preferred_element_type=jnp.float32) * scale
        bias = c[:, :, start:end, None] - c[:, :, None, :end]
        visible = jnp.arange(end)[None, :] <= jnp.arange(start, end)[:, None]
        p = jax.nn.softmax(jnp.where(visible, s + bias, -jnp.inf), axis=-1)
        outs.append(jnp.einsum('bhqk,bkhd->bqhd', p.astype(v.dtype), v[:, :end]))
    return jnp.concatenate(outs, axis=1)

def segsum(a):
    t = a.shape[-1]
    a_rep = jnp.broadcast_to(a[..., :, None], a.shape + (t,))
    a_rep = jnp.where(jnp.tril(jnp.ones((t, t), bool), -1), a_rep, 0.0)
    cs = jnp.cumsum(a_rep, axis=-2)
    return jnp.where(jnp.tril(jnp.ones((t, t), bool)), cs, -jnp.inf)

def ssd_chunked_scan(x, dt, a, bm, cm):
    b, L, h, p = x.shape
    g, n = bm.shape[2], bm.shape[3]
    e = h // g
    nc = L // SSD_CHUNK
    q = SSD_CHUNK
    xdt = (x * dt[..., None]).reshape(b, nc, q, g, e, p)
    da = (dt * a).reshape(b, nc, q, g, e).transpose(0, 3, 4, 1, 2)
    bc = bm.reshape(b, nc, q, g, n)
    cc = cm.reshape(b, nc, q, g, n)
    a_cum = jnp.cumsum(da, axis=-1)
    decay_in = jnp.exp(segsum(da))
    cb = jnp.einsum('bclgn,bcsgn->bgcls', cc, bc)
    y_diag = jnp.einsum('bgecls,bcsgep->bclgep', cb[:, :, None] * decay_in, xdt)
    decay_to_end = jnp.exp(a_cum[..., -1:] - a_cum).transpose(0, 3, 4, 1, 2)
    states = jnp.einsum('bclgn,bclgep->bcgepn', bc, xdt * decay_to_end[..., None])
    states = jnp.concatenate([jnp.zeros_like(states[:, :1]), states], axis=1)
    chunk_a = jnp.pad(a_cum[..., -1], [(0, 0), (0, 0), (0, 0), (1, 0)])
    chunk_decay = jnp.exp(segsum(chunk_a))
    prev_states = jnp.einsum('bgezc,bcgepn->bzgepn', chunk_decay, states)[:, :-1]
    decay_from_start = jnp.exp(a_cum).transpose(0, 3, 4, 1, 2)
    y_off = jnp.einsum('bclgn,bcgepn->bclgep', cc, prev_states) * decay_from_start[..., None]
    return (y_diag + y_off).reshape(b, L, h, p)

def mamba2_branch(z, xbc, dt, conv_w, conv_b, dt_bias, a_log, d_skip, norm_w):
    b, L, _ = z.shape
    f32 = jnp.float32
    xbc = jax.nn.silu(causal_depthwise_conv(xbc, conv_w, conv_b)).astype(f32)
    xs, bm, cm = jnp.split(xbc, [D_SSD, D_SSD + SSD_GROUPS * SSD_STATE], axis=-1)
    dt = jax.nn.softplus(dt.astype(f32) + dt_bias.astype(f32))
    a = -jnp.exp(a_log.astype(f32))
    xh = xs.reshape(b, L, SSD_HEADS, SSD_HEAD_DIM)
    y = ssd_chunked_scan(xh, dt, a,
                         bm.reshape(b, L, SSD_GROUPS, SSD_STATE),
                         cm.reshape(b, L, SSD_GROUPS, SSD_STATE))
    y = y + d_skip.astype(f32)[:, None] * xh
    gsz = D_SSD // SSD_GROUPS
    y = y.reshape(b, L, SSD_GROUPS, gsz) * jax.nn.silu(z.astype(f32)).reshape(b, L, SSD_GROUPS, gsz)
    y = y * lax.rsqrt(jnp.mean(y * y, axis=-1, keepdims=True) + NORM_EPS)
    return (y.reshape(b, L, D_SSD) * norm_w.astype(f32)).astype(z.dtype)

def rglru_branch(xr, gate, conv_w, conv_b, w_a, b_a, w_x, b_x, lam):
    b, L, _ = xr.shape
    f32 = jnp.float32
    xc = causal_depthwise_conv(xr, conv_w, conv_b).astype(f32)
    xb = xc.reshape(b, L, LRU_BLOCKS, LRU_BLOCK_DIM)
    r = jax.nn.sigmoid(jnp.einsum('blhi,hij->blhj', xb, w_a.astype(f32)).reshape(b, L, D_LRU) + b_a.astype(f32))
    i = jax.nn.sigmoid(jnp.einsum('blhi,hij->blhj', xb, w_x.astype(f32)).reshape(b, L, D_LRU) + b_x.astype(f32))
    log_a = LRU_C * r * jax.nn.log_sigmoid(lam.astype(f32))
    a = jnp.exp(log_a)
    mult = jnp.sqrt(-jnp.expm1(2.0 * log_a))
    mult = jnp.where(jnp.arange(L)[None, :, None] == 0, 1.0, mult)
    u = mult * (i * xc)

    def combine(left, right):
        a_l, u_l = left
        a_r, u_r = right
        return a_l * a_r, a_r * u_l + u_r

    _, hs = lax.associative_scan(combine, (a, u), axis=1)
    return (hs * jax.nn.gelu(gate.astype(f32))).astype(xr.dtype)

def mixer_block(h, w_in, fox_forget_bias, ssd_conv_w, ssd_conv_b, ssd_dt_bias, ssd_a_log, ssd_d, ssd_norm,
                lru_conv_w, lru_conv_b, lru_w_a, lru_b_a, lru_w_x, lru_b_x, lru_lambda,
                w_branch_attn, w_branch_ssd, w_branch_lru, w_out):
    b, L, _ = h.shape
    proj = h @ w_in
    q, k, v, f_logit, z, xbc, dt, xr, gate_r, merge = jnp.split(proj, _in_split_points(), axis=-1)
    log_f = jax.nn.log_sigmoid(f_logit.astype(jnp.float32) + fox_forget_bias.astype(jnp.float32))
    split_heads = lambda t: t.reshape(b, L, ATTN_HEADS, ATTN_HEAD_DIM)
    y_a = forgetting_attention(split_heads(q), split_heads(k), split_heads(v), log_f).reshape(b, L, D_ATTN)
    y_b = mamba2_branch(z, xbc, dt, ssd_conv_w, ssd_conv_b, ssd_dt_bias, ssd_a_log, ssd_d, ssd_norm)
    y_c = rglru_branch(xr, gate_r, lru_conv_w, lru_conv_b, lru_w_a, lru_b_a, lru_w_x, lru_b_x, lru_lambda)
    g_a, g_b, g_c = jnp.split(jax.nn.sigmoid(merge), N_BRANCH, axis=-1)
    mixed = g_a * (y_a @ w_branch_attn) + g_b * (y_b @ w_branch_ssd) + g_c * (y_c @ w_branch_lru)
    return mixed @ w_out

def setup_inputs(seed: int = 0) -> dict:
    key = jax.random.key(seed)
    keys = iter(jax.random.split(key, 40))

    def normal(shape, scale):
        return jax.random.normal(next(keys), shape, jnp.float32) * scale

    def uniform(shape, lo, hi):
        return jax.random.uniform(next(keys), shape, jnp.float32, lo, hi)

    def gain(shape):
        return 1.0 + normal(shape, 0.02)

    x = normal((BATCH, SEQ, D_MODEL), 1.0)
    meta_tokens = normal((N_META, D_MODEL), 1.0)
    ffn1_norm = gain((DEPTH, D_MODEL))
    ffn1_w_gate_up = normal((DEPTH, D_MODEL, 2 * D_FF), D_MODEL ** -0.5)
    ffn1_w_down = normal((DEPTH, D_FF, D_MODEL), D_FF ** -0.5)
    mix_norm = gain((DEPTH, D_MODEL))
    w_in = normal((DEPTH, D_MODEL, N_IN), D_MODEL ** -0.5)
    fox_forget_bias = FORGET_BIAS_INIT + normal((DEPTH, ATTN_HEADS), 0.5)
    ssd_conv_w = normal((DEPTH, SSD_CONV, D_XBC), SSD_CONV ** -0.5)
    ssd_conv_b = normal((DEPTH, D_XBC), 0.02)
    dt0 = jnp.exp(uniform((DEPTH, SSD_HEADS), math.log(1e-3), math.log(1e-1)))
    ssd_dt_bias = dt0 + jnp.log(-jnp.expm1(-dt0))
    ssd_a_log = jnp.log(uniform((DEPTH, SSD_HEADS), 1.0, 16.0))
    ssd_d = gain((DEPTH, SSD_HEADS))
    ssd_norm = gain((DEPTH, D_SSD))
    lru_conv_w = normal((DEPTH, LRU_CONV, D_LRU), LRU_CONV ** -0.5)
    lru_conv_b = normal((DEPTH, D_LRU), 0.02)
    lru_w_a = normal((DEPTH, LRU_BLOCKS, LRU_BLOCK_DIM, LRU_BLOCK_DIM), LRU_BLOCK_DIM ** -0.5)
    lru_b_a = normal((DEPTH, D_LRU), 0.02)
    lru_w_x = normal((DEPTH, LRU_BLOCKS, LRU_BLOCK_DIM, LRU_BLOCK_DIM), LRU_BLOCK_DIM ** -0.5)
    lru_b_x = normal((DEPTH, D_LRU), 0.02)
    a_pow_c = uniform((DEPTH, D_LRU), 0.9, 0.999)
    a0 = a_pow_c ** (1.0 / LRU_C)
    lru_lambda = jnp.log(a0) - jnp.log1p(-a0)
    w_branch_attn = normal((DEPTH, D_ATTN, D_MODEL), D_ATTN ** -0.5)
    w_branch_ssd = normal((DEPTH, D_SSD, D_MODEL), D_SSD ** -0.5)
    w_branch_lru = normal((DEPTH, D_LRU, D_MODEL), D_LRU ** -0.5)
    w_out = normal((DEPTH, D_MODEL, D_MODEL), D_MODEL ** -0.5)
    ffn2_norm = gain((DEPTH, D_MODEL))
    ffn2_w_gate_up = normal((DEPTH, D_MODEL, 2 * D_FF), D_MODEL ** -0.5)
    ffn2_w_down = normal((DEPTH, D_FF, D_MODEL), D_FF ** -0.5)
    final_norm = gain((D_MODEL,))
    return {'x': x, 'meta_tokens': meta_tokens,
            'ffn1_norm': ffn1_norm, 'ffn1_w_gate_up': ffn1_w_gate_up, 'ffn1_w_down': ffn1_w_down,
            'mix_norm': mix_norm, 'w_in': w_in, 'fox_forget_bias': fox_forget_bias,
            'ssd_conv_w': ssd_conv_w, 'ssd_conv_b': ssd_conv_b, 'ssd_dt_bias': ssd_dt_bias,
            'ssd_a_log': ssd_a_log, 'ssd_d': ssd_d, 'ssd_norm': ssd_norm,
            'lru_conv_w': lru_conv_w, 'lru_conv_b': lru_conv_b, 'lru_w_a': lru_w_a, 'lru_b_a': lru_b_a,
            'lru_w_x': lru_w_x, 'lru_b_x': lru_b_x, 'lru_lambda': lru_lambda,
            'w_branch_attn': w_branch_attn, 'w_branch_ssd': w_branch_ssd, 'w_branch_lru': w_branch_lru,
            'w_out': w_out,
            'ffn2_norm': ffn2_norm, 'ffn2_w_gate_up': ffn2_w_gate_up, 'ffn2_w_down': ffn2_w_down,
            'final_norm': final_norm}

def reference(x, meta_tokens, ffn1_norm, ffn1_w_gate_up, ffn1_w_down, mix_norm, w_in, fox_forget_bias,
              ssd_conv_w, ssd_conv_b, ssd_dt_bias, ssd_a_log, ssd_d, ssd_norm,
              lru_conv_w, lru_conv_b, lru_w_a, lru_b_a, lru_w_x, lru_b_x, lru_lambda,
              w_branch_attn, w_branch_ssd, w_branch_lru, w_out,
              ffn2_norm, ffn2_w_gate_up, ffn2_w_down, final_norm):
    b, s, d = x.shape
    length = N_META + s
    padded = -(-length // Q_BLOCK) * Q_BLOCK
    meta = jnp.broadcast_to(meta_tokens.astype(x.dtype)[None], (b, N_META, d))
    h = jnp.concatenate([meta, x, jnp.zeros((b, padded - length, d), x.dtype)], axis=1)
    for l in range(DEPTH):
        h = h + 0.5 * swiglu_ffn(rms_norm(h, ffn1_norm[l]), ffn1_w_gate_up[l], ffn1_w_down[l])
        h = h + mixer_block(rms_norm(h, mix_norm[l]), w_in[l], fox_forget_bias[l],
                            ssd_conv_w[l], ssd_conv_b[l], ssd_dt_bias[l], ssd_a_log[l], ssd_d[l], ssd_norm[l],
                            lru_conv_w[l], lru_conv_b[l], lru_w_a[l], lru_b_a[l], lru_w_x[l], lru_b_x[l],
                            lru_lambda[l], w_branch_attn[l], w_branch_ssd[l], w_branch_lru[l], w_out[l])
        h = h + 0.5 * swiglu_ffn(rms_norm(h, ffn2_norm[l]), ffn2_w_gate_up[l], ffn2_w_down[l])
    return rms_norm(h, final_norm)[:, N_META:N_META + s]


_drawn_inputs = setup_inputs


def setup_inputs(seed=0):
    import zlib

    import numpy as np

    out = dict(_drawn_inputs(seed))
    spreads = {}
    factors = {'ffn1_norm': 5.622,
     'mix_norm': 3.384,
     'ssd_conv_b': 20.688,
     'ssd_d': 200.0,
     'ssd_norm': 38.732,
     'lru_b_a': 47.81,
     'lru_b_x': 35.47,
     'ffn2_norm': 24.64,
     'final_norm': 20.501,
     'lru_conv_b': 4.771,
     'fox_forget_bias': 3.187}
    for name, (base, spread) in spreads.items():
        noise = np.random.default_rng([zlib.crc32(name.encode()), seed]).standard_normal(out[name].shape)
        drawn = base * np.exp(spread * noise) if base else spread * noise
        out[name] = __import__('jax').numpy.asarray(drawn.astype(out[name].dtype))
    for name, factor in factors.items():
        out[name] = (out[name] * factor).astype(out[name].dtype)
    return out
```

```python
from contextlib import ExitStack

import numpy as np

import concourse.bass as bass
from concourse import mybir

F32 = mybir.dt.float32
F32R = mybir.dt.float32r
BF16 = mybir.dt.bfloat16
ALU = mybir.AluOpType
ACT = mybir.ActivationFunctionType
AX_X = mybir.AxisListType.X

P = 128
RING = 3
KC = 8
SLAB = KC * 2 * P
NEG = -1.0e30
GELU_C = 0.044715
GELU_S = float(np.sqrt(2.0 / np.pi))
EPS = 1e-6
LN_EXP = "natural_log_exp_and_others"
EXP_TANH = "exp_and_others"


class Own:

    def __init__(self, eng, sem):
        self.eng, self.sem, self.n = eng, sem, 0

    def did(self, ins):
        ins.then_inc(self.sem, 1)
        self.n += 1
        return self.n

    def settle(self, n=None):
        self.eng.wait_ge(self.sem, self.n if n is None else n)


def hybrid_trunk(nc, a, out):
    D = a["x"].shape[2]
    SEQ = a["x"].shape[1]
    META = a["meta_tokens"].shape[0]
    T = META + SEQ
    TQ = SEQ
    DFF = a["ffn1_w_down"].shape[1]
    C = D // P
    FC = DFF // P
    H = a["ssd_d"].shape[1]
    DH = D // H
    assert (D, SEQ, META, H, DH, FC) == (1024, 256, 16, 16, 64, 22)
    ALL = slice(0, T)
    OUTS = slice(META, T)
    T0 = slice(META, META + P)
    T1 = slice(META + P, T)

    w_in = a["w_in"][0]
    sizes = [D, D, D, H, D, D + 2 * 2 * P, H, D, D, 3 * D]
    starts = [int(v) for v in np.cumsum([0] + sizes)]
    oq, ok, ov, of, oz, oxbc, odt, oxr, ogate, omerge = starts[:10]

    GU1 = 0
    DN1 = GU1 + FC
    FIRST = DN1 + 12
    XR = [FIRST, FIRST + 2, FIRST + 4, FIRST + 6]
    GATE = [n + 1 for n in XR]
    FDT = GATE[3] + 1
    XBC = FDT + 1
    LRU_AT = [n + 1 for n in XR]
    ZZ = XBC + 6
    QQ = ZZ + 4
    KK = QQ + 4
    VV = KK + 4
    MG = VV + 4
    WO = MG + 24
    GU2 = WO + 4
    DN2 = GU2 + FC
    END = DN2 + 12
    SCAN_AT = [LRU_AT[1] + 1, ZZ]
    YC_AT = [ZZ, ZZ + 1]
    LOADS = [1] * END
    for n in [FDT, *range(GU1, DN1), *range(MG, WO), *range(GU2, DN2)]:
        LOADS[n] = 2
    ORDER = [2, 1, 0]
    YT_AT = {MG + 8: 0, MG + 9: 1, MG + 12: 2, MG + 15: 3}

    def arrived(n):
        return 16 * sum(LOADS[n % RING:n + 1:RING])

    def width(n):
        for d in (DN1, DN2):
            if d <= n < d + 12 and (n - d) % 3 == 2:
                return (FC - 16) * 2 * P
        return SLAB

    with ExitStack() as ctx:
        def sb(name, shape, dt=F32, st=ctx):
            return st.enter_context(nc.sbuf_tensor(name, shape, dt))

        def sem(name):
            return ctx.enter_context(nc.semaphore(name))

        raw = sb("raw", [P, RING, SLAB])
        whi = sb("whi", [P, RING, SLAB], F32R)
        wlo = sb("wlo", [P, RING, SLAB], F32R)
        xres = sb("xres", [P, C, T])
        thi = sb("act_hi", [P, C, T], F32R)
        tlo = sb("act_lo", [P, C, T], F32R)
        hn = sb("hn", [P, RING, T])
        acc = sb("acc", [P, T])
        rstd = sb("rstd", [P, T])
        ident = sb("ident", [P, P])
        ones = sb("ones", [P, P])
        sel = sb("sel", [48, 48], F32R)
        identb = sb("identb", [P, P], BF16)
        mask_qk = sb("mask_qk", [P, P], BF16)
        mask_st = sb("mask_st", [P, P], BF16)
        colA = sb("colA", [P, 100])
        colB = sb("colB", [P, 64])
        small = sb("small", [P, 48])
        eps = sb("eps", [P, 1])
        dcol = sb("dcol", [P, C])
        scl48 = sb("scl48", [48, 4])

        with ExitStack() as s1:
            sq = sb("sq", [P, C, T], F32, s1)
            tokio = sb("tokio", [P, 2, D], F32, s1)
            metain = sb("metain", [META, D], F32, s1)
            rows = sb("rows", [P, 2, P], F32, s1)
            stmp = sb("stmp", [P, RING, T], F32, s1)
            hid_hi = sb("hid_hi", [P, FC, T], F32R, s1)
            hid_lo = sb("hid_lo", [P, FC, T], F32R, s1)

        XC = sb("xc_kt", [P, C, T])
        G = sb("gelu_qt", [P, C, TQ])
        XBCV = sb("xbc_v", [P, 12, T])
        Z = sb("z_mix", [P, C, TQ])
        XDV = sb("xdt_ytok", [P, 3 * D])
        y0hi = sb("y0hi", [P, C, TQ], F32R)
        y0lo = sb("y0lo", [P, C, TQ], F32R)
        craw = sb("craw", [P, 2, 2, T + 3])
        th = sb("th", [P, 2, T])
        work = sb("work", [P, 2560])
        cs_hi = sb("cs_hi", [48, T], F32R)
        cs_lo = sb("cs_lo", [48, T], F32R)
        tokm = sb("tokm", [P, 192])
        toka = sb("toka", [META, 96])
        with ExitStack() as s2:
            y1hi = sb("y1hi", [P, C, TQ], F32R, s2)
            y1lo = sb("y1lo", [P, C, TQ], F32R, s2)
        with ExitStack() as s3:
            bda = sb("bda", [P, C, P], F32, s3)
            bdx = sb("bdx", [P, C, P], F32, s3)
            la = sb("la", [P, 4, T], F32, s3)

        KT, QT = XC, G
        XT = XBCV
        V = XBCV[:, :, :].rearrange("p c t -> p (c t)")
        VM = V[:, 0:2 * D].rearrange("p (j d) -> p j d", j=2)
        VA = V[0:META, 2 * D:3 * D]
        XDM = XDV[:, 0:2 * D].rearrange("p (j d) -> p j d", j=2)
        XDA = XDV[0:META, 2 * D:3 * D]
        YTOK = XDM
        MIX = Z
        xt48, e48, u48, l48, one48, sp48, cs48 = (XDV[0:48, k * T:(k + 1) * T] for k in range(7))
        thr = work[:, 0:2 * T].rearrange("p (j t) -> p j t", j=2)
        thx = work[:, 2 * T:4 * T].rearrange("p (j t) -> p j t", j=2)
        lv = work[:, 4 * T:8 * T].rearrange("p (j t) -> p j t", j=4)
        CB = work[:, 0:768].rearrange("p (g t) -> p g t", g=2)
        CBA = work[0:META, 768:1280].rearrange("p (g t) -> p g t", g=2)
        E = work[:, 1280:2048].rearrange("p (b t) -> p b t", b=2)
        EA = work[0:META, 2048:2560].rearrange("p (b t) -> p b t", b=2)
        PR = work[:, 0:832].rearrange("p (b t) -> p b t", b=2)
        PT = work[:, 832:1600].rearrange("p (b t) -> p b t", b=2)
        PTA = work[0:META, 1600:2112].rearrange("p (b t) -> p b t", b=2)
        RS = work[:, 2112:2144]
        NM = work[:, 2144:2176]
        RI = work[:, 2176:2208]
        crf = craw[:, :, :, :].rearrange("p a b t -> p (a b t)")
        ytmp, ysq = crf[:, 0:TQ], crf[:, TQ:2 * TQ]
        mt = hn

        cA = {}
        at = 0
        for name, k in (("ffn1_norm", 8), ("mix_norm", 8), ("ffn2_norm", 8), ("final_norm", 8), ("ssd_norm", 8),
                        ("ssd_conv_b", 12), ("ssd_conv_w", 48)):
            cA[name] = at
            at += k
        nA = at
        cB = {}
        at = 0
        for name, k in (("lru_conv_w", 32), ("lru_conv_b", 8), ("lru_b_a", 8), ("lru_b_x", 8), ("lru_lambda", 8)):
            cB[name] = at
            at += k
        nB = at

        def col(name, k):
            return (colA[:, cA[name] + k:cA[name] + k + 1] if name in cA else
                    colB[:, cB[name] + k:cB[name] + k + 1])

        ba2, bx2, cpos, cneg, lam_e, lam_l = (small[:, 8 * k:8 * k + 8] for k in range(6))
        lam = colB[:, cB["lru_lambda"]:cB["lru_lambda"] + 8]

        banks = ctx.enter_context(nc.psum_tensor("banks", [P, 8, 512], F32))

        raw_in = [sem(f"raw_in{s}") for s in range(RING)]
        hi_done = sem("hi_done")
        lo_done = sem("lo_done")
        tiles_done = sem("tiles_done")
        evac = [sem("evac0"), sem("evac1")]
        x_in = sem("x_in")
        vec_in = sem("vec_in")
        lru_w_in = sem("lru_w_in")
        sml_in = sem("sml_in")
        consts = sem("consts")
        eps_set = sem("eps_set")
        scl_zero = sem("scl_zero")
        scl_ready = sem("scl_ready")
        lru_p = sem("lru_p")
        bd_zero = sem("bd_zero")
        pool_own = sem("pool_own")
        act_own = sem("act_own")
        dve_own = sem("dve_own")
        xt_done = sem("xt_done")
        vt_done = sem("vt_done")
        cols_done = sem("cols_done")
        x_new = sem("x_new")
        sq_done = sem("sq_done")
        sq_sum = sem("sq_sum")
        stat_done = sem("stat_done")
        rstd_done = sem("rstd_done")
        hn_done = sem("hn_done")
        nhi_done = sem("nhi_done")
        act_ready = sem("act_ready")
        silu_done = sem("silu_done")
        h_done = sem("h_done")
        hhi_done = sem("hhi_done")
        hlo_done = sem("hlo_done")
        lam_act = sem("lam_act")
        lam_dve = sem("lam_dve")
        fdt_act = sem("fdt_act")
        fdt_dve = sem("fdt_dve")
        fdt_tr = sem("fdt_tr")
        tok_ready = sem("tok_ready")
        cs_rounded = sem("cs_rounded")
        cs_split = sem("cs_split")
        sel_done = sem("sel_done")
        conv_done = sem("conv_done")
        lru_mm = sem("lru_mm")
        lru_acted = sem("lru_acted")
        gate_arg = sem("gate_arg")
        gate_th = sem("gate_th")
        gate_done = sem("gate_done")
        lru_a = sem("lru_a")
        lru_v = sem("lru_v")
        lru_mult = sem("lru_mult")
        lru_scan = sem("lru_scan")
        lru_h = sem("lru_h")
        yc_hi = sem("yc_hi")
        yc_ready = sem("yc_ready")
        xbc_th = sem("xbc_th")
        xbc_ready = sem("xbc_ready")
        z_th = sem("z_th")
        x_tr = sem("x_tr")
        xdt_done = sem("xdt_done")
        cb_mm = sem("cb_mm")
        cb_done = sem("cb_done")
        dec_mm = sem("dec_mm")
        dec_exp = sem("dec_exp")
        w_done = sem("w_done")
        y_done = sem("y_done")
        y_evac = sem("y_evac")
        ysq_done = sem("ysq_done")
        gstat = sem("gstat")
        grs_done = sem("grs_done")
        yb_scaled = sem("yb_scaled")
        yb_hi = sem("yb_hi")
        yb_ready = sem("yb_ready")
        v_tr = sem("v_tr")
        v_main = sem("v_main")
        v_meta = sem("v_meta")
        s_mm = sem("s_mm")
        s_max = sem("s_max")
        s_exp = sem("s_exp")
        p_tr = sem("p_tr")
        pt_main = sem("pt_main")
        pt_meta = sem("pt_meta")
        av_mm = sem("av_mm")
        ytok_done = sem("ytok_done")
        ya_tr = sem("ya_tr")
        ya_hi = sem("ya_hi")
        ya_ready = sem("ya_ready")
        mg_th = sem("mg_th")
        mix_new = sem("mix_new")
        mix_hi = sem("mix_hi")
        mix_ready = sem("mix_ready")
        o_tr = sem("o_tr")
        o_act = sem("o_act")
        o_dve = sem("o_dve")
        stored = sem("stored")

        def rounds(eng, first, count, step):
            turns = count // RING
            if turns > 1:
                with eng.Fori(0, turns) as i:
                    for j in range(RING):
                        step(i * RING + (first + j), (first + j) % RING,
                         i * (16 * LOADS[first]) + arrived(first + j), i, j)
            else:
                turns = 0
            for n in range(first + RING * turns, first + count):
                step(n, n % RING, arrived(n), (n - first) // RING, (n - first) % RING)

        def pj(n):
            return 2 * (n % 2)

        def freed(n):
            return (n - FIRST) // 2 + 1

        def attn_lo(dve, g):
            dve.wait_ge(ya_hi, g + 1)
            dve.tensor_tensor(y0lo[:, 2 * g:2 * g + 2, :], banks[:, 5, :].rearrange("p (c t) -> p c t", c=2),
                              y0hi[:, 2 * g:2 * g + 2, :].bitcast(F32), ALU.subtract).then_inc(ya_ready, 1)

        def attn_turn(pe, g, before):
            pe.wait_ge(ytok_done, g + 1)
            pe.wait_ge(pt_meta, before)
            for c in range(2):
                for j in range(2):
                    last = pe.transpose(banks[:, 5, 2 * P * c + P * j:2 * P * c + P * (j + 1)],
                                        YTOK[:, j, 2 * P * g + P * c:2 * P * g + P * (c + 1)], ident[:, :])
            last.then_inc(ya_tr, 1)

        def attn_values(pe, h):
            b, o = h % 2, P * (h % 4)
            hs = slice(DH * h, DH * (h + 1))
            pe.wait_ge(pt_main, h + 1)
            pe.wait_ge(pt_meta, h + 1)
            if h == 0:
                pe.wait_ge(v_main, 4)
                pe.wait_ge(v_meta, 4)
            elif h % 4 == 0:
                pe.wait_ge(ytok_done, h // 4)
            y0, y1 = banks[:, 4, o:o + DH], banks[:, 4, o + DH:o + P]
            pe.matmul(y0, PTA[:, b, 0:P], VA[:, hs], start=True, stop=False)
            pe.matmul(y0, PT[:, b, 0:P], VM[:, 0, hs], start=False, stop=False)
            pe.matmul(y1, PTA[:, b, P:2 * P], VA[:, hs], start=False, stop=False)
            pe.matmul(y1, PT[:, b, P:2 * P], VM[:, 0, hs], start=False, stop=False)
            pe.matmul(y1, PT[:, b, 2 * P:3 * P], VM[:, 1, hs], start=False, stop=True).then_inc(av_mm, 1)

        def to_tokens(pe, src):
            for c in range(2):
                for j, ts in enumerate((T0, T1)):
                    pe.transpose(banks[:, 4, 2 * P * c + P * j:2 * P * c + P * (j + 1)], src(c, ts), ident[:, :])
                last = pe.transpose(banks[0:META, 5, P * c:P * (c + 1)], src(c, slice(0, META)), ident[:, :])
            return last

        block = ctx.enter_context(nc.Block())

        @block.sync
        def _(sp):
            def dst(slot, kcs=KC):
                return raw[:, slot, 0:kcs * 2 * P].rearrange("p (c n) -> p c n", c=kcs)

            def reuse(n):
                sp.wait_ge(lo_done, n + 1 - RING)

            def vectors():
                for tile, cols, names in ((0, cA, ("ffn1_norm", "mix_norm", "ffn2_norm", "final_norm", "ssd_norm",
                                                   "ssd_conv_b", "ssd_conv_w")),
                                          (1, cB, ("lru_conv_w", "lru_conv_b", "lru_b_a", "lru_b_x", "lru_lambda"))):
                    for name in names:
                        v = a[name]
                        if name == "final_norm":
                            src = v.rearrange("(c p) -> c p", p=P)
                        elif v.ndim == 3:
                            src = v[0].rearrange("k (c p) -> (k c) p", p=P)
                        else:
                            src = v[0].rearrange("(c p) -> c p", p=P)
                        sp.dma_start(rows[cols[name]:cols[name] + src.shape[0], tile, :], src).then_inc(vec_in, 16)
                sp.wait_ge(scl_zero, 1)
                sp.dma_start(scl48[0:H, 0:1], a["fox_forget_bias"].rearrange("a h -> h a"),
                              allow_slow_non_contiguous=True).then_inc(sml_in, 16)
                sp.dma_start(scl48[32:48, 0:1], a["ssd_dt_bias"].rearrange("a h -> h a"),
                              allow_slow_non_contiguous=True).then_inc(sml_in, 16)
                sp.dma_start(scl48[32:48, 2:3], a["ssd_a_log"].rearrange("a h -> h a"),
                              allow_slow_non_contiguous=True).then_inc(sml_in, 16)
                for two in range(2):
                    sp.dma_start(dcol[DH * two:DH * (two + 1), :],
                                  a["ssd_d"].rearrange("a (c two) -> a two c", two=2)[:, two].broadcast_to([DH, C]),
                                  allow_slow_non_contiguous=True)\
                       .then_inc(sml_in, 16)

            def ffn(w_gu, w_dn, first, peel):
                gu = w_gu.rearrange("(c p) (two f) -> p c two f", p=P, two=2)
                dn = w_dn.rearrange("(c p) n -> p c n", p=P)

                def gate_up(n, slot, _arr, turn, j, base=first):
                    m = n - base
                    if not (isinstance(n, int) and n < RING):
                        reuse(n)
                    for two in range(2):
                        sp.dma_start(dst(slot)[:, :, two * P:(two + 1) * P], gu[:, :, two, bass.ds(m * P, P)])\
                          .then_inc(raw_in[slot], 16)

                for n in range(first, first + peel):
                    gate_up(n, n % RING, 0, 0, 0)
                    if n == 0:
                        vectors()
                rounds(sp, first + peel, FC - peel, gate_up)

                def down(n, slot, _arr, turn, j):
                    kcs = FC - 16 if j == 2 else KC
                    reuse(n)
                    sp.dma_start(dst(slot, kcs), dn[:, 8 * j:8 * j + kcs, bass.ds(turn * 2 * P, 2 * P)])\
                      .then_inc(raw_in[slot], 16)

                rounds(sp, first + FC, 12, down)

            ffn(a["ffn1_w_gate_up"][0], a["ffn1_w_down"][0], GU1, RING)

            win = w_in.rearrange("(c p) n -> p c n", p=P)

            def load(n, src):
                reuse(n)
                sp.dma_start(dst(n % RING), src).then_inc(raw_in[n % RING], 16)

            sources = {}
            for slabs, o in ((XR, oxr), (GATE, ogate), (range(XBC, ZZ), oxbc), (range(ZZ, QQ), oz),
                             (range(QQ, KK), oq), (range(KK, VV), ok), (range(VV, MG), ov)):
                for j, n in enumerate(slabs):
                    sources[n] = o + 2 * P * j
            for n in range(FIRST, MG):
                if n == FDT:
                    reuse(n)
                    for at, o in ((0, of), (32, odt)):
                        sp.dma_start(dst(n % RING)[:, :, at:at + H], win[:, :, o:o + H]).then_inc(raw_in[n % RING], 16)
                else:
                    load(n, win[:, :, sources[n]:sources[n] + 2 * P])
            branch = [a["w_branch_attn"][0], a["w_branch_ssd"][0], a["w_branch_lru"][0]]
            for k in range(24):
                b, m, n = ORDER[k // C], k % C, MG + k
                reuse(n)
                sp.dma_start(dst(n % RING)[:, :, 0:P], win[:, :, omerge + b * D + m * P:omerge + b * D + (m + 1) * P])\
                  .then_inc(raw_in[n % RING], 16)
                sp.dma_start(dst(n % RING)[:, :, P:2 * P],
                             branch[b].rearrange("(c p) n -> p c n", p=P)[:, :, m * P:(m + 1) * P])\
                  .then_inc(raw_in[n % RING], 16)
            for j in range(4):
                load(WO + j, a["w_out"][0].rearrange("(c p) n -> p c n", p=P)[:, :, 2 * P * j:2 * P * (j + 1)])
            ffn(a["ffn2_w_gate_up"][0], a["ffn2_w_down"][0], GU2, 0)

            for half in range(2):
                sp.wait_ge(o_dve, half + 1)
                sp.wait_ge(o_act, half + 1)
                sp.dma_start(out[0].rearrange("(j p) d -> p j d", p=P)[:, :, 512 * half:512 * (half + 1)],
                             tokio[:, :, 512 * half:512 * (half + 1)]).then_inc(stored, 16)
            sp.wait_ge(stored, 32)

        @block.gpsimd
        def _(pool):
            own = Own(pool, pool_own)
            own.did(pool.memset(ident[:, :], 0.0))
            own.did(pool.memset(mask_qk[:, :], 0.0))
            own.did(pool.memset(mask_st[:, :], 0.0))
            pool.memset(ones[:, :], 1.0).then_inc(consts, 1)
            own.settle()
            own.did(pool.affine_select(out=ident[:, :], in_=ident[:, :], pattern=[[-1, P]],
                                       compare_op=ALU.not_equal, fill=1.0, base=0, channel_multiplier=1))
            pool.affine_select(out=mask_qk[:, :], in_=mask_qk[:, :], pattern=[[-1, P]],
                               compare_op=ALU.is_ge, fill=NEG, base=0, channel_multiplier=1).then_inc(consts, 1)
            pool.affine_select(out=mask_st[:, :], in_=mask_st[:, :], pattern=[[1, P]],
                               compare_op=ALU.is_ge, fill=NEG, base=0, channel_multiplier=-1).then_inc(consts, 1)
            own.settle()
            pool.tensor_copy(identb[:, :], ident[:, :]).then_inc(consts, 1)
            pool.tensor_copy(sel[:, :], ident[0:48, 0:48]).then_inc(sel_done, 1)
            pool.memset(bda[:, :, :], 0.0).then_inc(bd_zero, 1)
            pool.memset(bdx[:, :, :], 0.0).then_inc(bd_zero, 1)
            pool.wait_ge(bd_zero, 2)
            for bd, w in ((bda, a["lru_w_a"][0]), (bdx, a["lru_w_x"][0])):
                for two in range(2):
                    pool.dma_start(bd[DH * two:DH * (two + 1), :, DH * two:DH * (two + 1)],
                                   w.rearrange("(t two) i j -> i two t j", two=2)[:, two]).then_inc(lru_w_in, 16)

            def sum_squares(q, cols):
                for k in range(3):
                    pool.wait_ge(sq_done, 4 * q + k + 1)
                    for c in (2 * k, 2 * k + 1):
                        if c == 0:
                            continue
                        if c == 1 and q > 0:
                            pool.wait_ge(stat_done, q)
                        if c == 1 and q == 2:
                            pool.wait_ge(yb_scaled, 2)
                        first = sq[:, 0, cols] if c == 1 else acc[:, cols]
                        ins = pool.tensor_tensor(acc[:, cols], first, sq[:, c, cols], ALU.add)
                        if c == 5:
                            ins.then_inc(sq_sum, 1)
                        else:
                            own.did(ins)
                            own.settle()

            sum_squares(0, ALL)
            sum_squares(1, ALL)
            sum_squares(2, OUTS)
            sum_squares(3, OUTS)

        @block.scalar
        def _(act):
            own = Own(act, act_own)

            act.dma_start(tokio[:, :, :], a["x"][0].rearrange("(j p) d -> p j d", p=P)).then_inc(x_in, 16)
            act.dma_start(metain[:, :], a["meta_tokens"]).then_inc(x_in, 16)

            def split(n, slot, arr, w):
                act.wait_ge(raw_in[slot], arr)
                if not (isinstance(n, int) and n < RING):
                    act.wait_ge(tiles_done, 2 * (n - RING) + 2)
                act.activation(whi[:, slot, 0:w], raw[:, slot, 0:w], ACT.Copy).then_inc(hi_done, 1)

            def split_at(n):
                if n < END:
                    split(n, n % RING, arrived(n), width(n))

            def squares(q, k, cols):
                act.wait_ge(x_new, C * q + 2 * k + 2)
                act.activation(sq[:, 2 * k:2 * k + 2, cols], xres[:, 2 * k:2 * k + 2, cols], ACT.Square)\
                   .then_inc(sq_done, 1)

            def norm(q, cols):
                act.preload_act_table_set(LN_EXP)
                act.wait_ge(stat_done, q + 1)
                own.did(act.activation(rstd[:, cols], banks[:, 7, 0:cols.stop - cols.start], ACT.Ln,
                                       bias=eps[:, 0:1], scale=1.0 / D))
                own.settle()
                act.activation(rstd[:, cols], rstd[:, cols], ACT.Exp, scale=-0.5).then_inc(rstd_done, 1)
                if q < 3:
                    for c in range(C):
                        act.wait_ge(hn_done, C * q + c + 1)
                        act.activation(thi[:, c, cols], hn[:, c % RING, cols], ACT.Copy).then_inc(nhi_done, 1)

            for k in range(4):
                squares(0, k, ALL)
            split_at(0)
            act.wait_ge(eps_set, 1)
            norm(0, ALL)
            for n in range(1, RING):
                split_at(n)
            own.did(act.activation(lam_e, lam, ACT.Abs))
            own.settle()
            act.activation(lam_e, lam_e, ACT.Exp, scale=-1.0).then_inc(lam_act, 1)
            act.wait_ge(sml_in, 80)
            act.activation(scl48[32:48, 3:4], scl48[32:48, 2:3], ACT.Exp).then_inc(lam_act, 1)
            act.wait_ge(lam_dve, 1)
            act.activation(lam_l, cpos, ACT.Ln).then_inc(lam_act, 1)

            def ffn(q, first, cols, base):
                w = cols.stop - cols.start

                def gate_up(n, slot, arr, turn, j, wide=None, m=None):
                    m = n - first if m is None else m
                    act.wait_ge(tiles_done, 2 * n + 1)
                    if not (isinstance(n, int) and n < RING):
                        act.wait_ge(h_done, m + (base - RING + 1))
                    act.activation(stmp[:, slot, 0:w], banks[:, 2 * slot, 0:w], ACT.Silu).then_inc(silu_done, 1)
                    nxt = arrived(n + RING) if isinstance(n, int) else arr + 16 * LOADS[first]
                    split(n + RING, slot, nxt, SLAB if wide is None else wide)
                    act.wait_ge(h_done, m + (base + 1))
                    act.activation(hid_hi[:, m, cols] if isinstance(m, int) else hid_hi[:, bass.ds(m, 1), cols],
                                   (hn[:, slot, 0:w] if isinstance(m, int) else hn[:, slot:slot + 1, 0:w]),
                                   ACT.Copy).then_inc(hhi_done, 1)

                peel = RING if first == 0 else 0
                for n in range(first, first + peel):
                    gate_up(n, n % RING, arrived(n), 0, 0)
                rounds(act, first + peel, FC - RING - peel, gate_up)
                for n in range(first + FC - RING, first + FC):
                    gate_up(n, n % RING, arrived(n), 0, 0, wide=width(n + RING))

                d0 = first + FC

                def down(n, slot, arr, turn, j, ahead=True):
                    if j == 2:
                        squares_dyn(turn)
                    if ahead:
                        split(n + RING, slot, arr + 16, (FC - 16) * 2 * P if j == 2 else SLAB)

                def squares_dyn(turn):
                    act.wait_ge(x_new, turn * 2 + (C * q + 2))
                    if isinstance(turn, int):
                        o, i = sq[:, 2 * turn:2 * turn + 2, cols], xres[:, 2 * turn:2 * turn + 2, cols]
                    else:
                        o, i = sq[:, bass.ds(turn * 2, 2), cols], xres[:, bass.ds(turn * 2, 2), cols]
                    act.activation(o, i, ACT.Square).then_inc(sq_done, 1)

                rounds(act, d0, 9, down)
                for j in range(RING):
                    down(d0 + 9 + j, (d0 + 9 + j) % RING, 0, 3, j, ahead=False)
                    if j < 2:
                        split_at(d0 + 12 + j)

            ffn(1, GU1, ALL, 0)
            norm(1, ALL)
            split_at(FIRST + 2)

            def conv_evac(n, i, name_w, name_b, c0, dest, stride):
                if i >= 2:
                    act.wait_ge(conv_done, i - 1)
                for t in range(2):
                    act.activation(dest[:, c0 + t, :], banks[:, pj(n) + t, 0:T], ACT.Identity,
                                   scale=col(name_w, 3 * stride + c0 + t), bias=col(name_b, c0 + t))
                    ins = act.activation(craw[:, i % 2, t, 3:3 + T], banks[:, pj(n) + t, 0:T], ACT.Copy)
                ins.then_inc(evac[n % 2], 1)

            def decay_exps(i):
                for b in range(2):
                    h = 2 * i + b
                    act.wait_ge(dec_mm, h + 1)
                    if i > 0:
                        act.wait_ge(y_done, i)
                    act.activation(E[:, b, 0:2 * P], banks[:, 4 + b, 0:2 * P], ACT.Exp,
                                   bias=tokm[:, 128 + h:129 + h])
                    act.activation(E[:, b, 2 * P:3 * P], banks[:, 4 + b, 3 * P:4 * P], ACT.Exp,
                                   bias=tokm[:, 176 + h:177 + h])
                    act.activation(EA[:, b, :], banks[0:META, 4 + b, P:3 * P], ACT.Exp,
                                   bias=toka[:, 80 + h:81 + h]).then_inc(dec_exp, 1)

            for n in range(FIRST, GU2):
                act.wait_ge(tiles_done, 2 * n + 2)
                if n == FDT:
                    act.wait_ge(scl_ready, 1)
                    act.activation(xt48, banks[0:48, pj(n), 0:T], ACT.Identity, scale=scl48[:, 1:2],
                                   bias=scl48[:, 0:1]).then_inc(evac[n % 2], 1)
                elif n in XR:
                    conv_evac(n, XR.index(n), "lru_conv_w", "lru_conv_b", 2 * XR.index(n), XC, C)
                elif n in GATE:
                    j = GATE.index(n)
                    if j > 0:
                        act.wait_ge(gate_done, j)
                    src = banks[:, pj(n):pj(n) + 2, 0:TQ]
                    act.activation(th[:, :, 0:TQ], src, ACT.Square, scale=float(np.sqrt(GELU_C)))
                    act.activation(G[:, 2 * j:2 * j + 2, :], src, ACT.Copy).then_inc(evac[n % 2], 1)
                elif XBC <= n < ZZ:
                    conv_evac(n, 4 + n - XBC, "ssd_conv_w", "ssd_conv_b", 2 * (n - XBC), XT, 12)
                elif ZZ <= n < QQ:
                    j = n - ZZ
                    act.activation(Z[:, 2 * j:2 * j + 2, :], banks[:, pj(n):pj(n) + 2, 0:TQ], ACT.Tanh, scale=0.5)\
                       .then_inc(z_th, 1)
                elif QQ <= n < KK:
                    j = n - QQ
                    act.wait_ge(yc_ready, 2)
                    act.activation(QT[:, 2 * j:2 * j + 2, :], banks[:, pj(n):pj(n) + 2, 0:TQ], ACT.Copy,
                                   scale=float(DH) ** -0.5).then_inc(evac[n % 2], 1)
                elif KK <= n < VV:
                    j = n - KK
                    act.activation(KT[:, 2 * j:2 * j + 2, :], banks[:, pj(n):pj(n) + 2, 0:T], ACT.Copy)\
                       .then_inc(evac[n % 2], 1)
                elif VV <= n < MG:
                    j = n - VV
                    if j > 0:
                        act.wait_ge(v_tr, j)
                    else:
                        act.wait_ge(xbc_ready, 6)
                    act.activation(th[:, :, :], banks[:, pj(n):pj(n) + 2, 0:T], ACT.Copy).then_inc(evac[n % 2], 1)
                elif MG <= n < WO:
                    k = n - MG
                    if k >= 2:
                        act.wait_ge(evac[n % 2], freed(n - 2))
                    act.activation(mt[:, k % 2, 0:TQ], banks[:, pj(n), 0:TQ], ACT.Tanh, scale=0.5)\
                       .then_inc(mg_th, 1)

                if n in YT_AT:
                    g = YT_AT[n]
                    act.wait_ge(ya_tr, g + 1)
                    act.activation(y0hi[:, 2 * g:2 * g + 2, :], banks[:, 5, :].rearrange("p (c t) -> p c t", c=2),
                                   ACT.Copy).then_inc(ya_hi, 1)
                if n == FDT:
                    act.preload_act_table_set(LN_EXP)
                    act.wait_ge(evac[FDT % 2], freed(FDT))
                    own.did(act.activation(e48, xt48, ACT.Abs))
                    own.settle()
                    act.activation(e48, e48, ACT.Exp, scale=-1.0).then_inc(fdt_act, 1)
                    act.wait_ge(fdt_dve, 1)
                    act.activation(l48, u48, ACT.Ln).then_inc(fdt_act, 1)
                if n == FDT + 2:
                    act.wait_ge(fdt_dve, 2)
                    act.activation(cs_hi[:, :], cs48, ACT.Copy).then_inc(cs_rounded, 1)
                if n in GATE:
                    act.wait_ge(gate_arg, GATE.index(n) + 1)
                    act.activation(th[:, :, 0:TQ], th[:, :, 0:TQ], ACT.Tanh, scale=GELU_S).then_inc(gate_th, 1)
                if n in SCAN_AT:
                    half = SCAN_AT.index(n)
                    act.preload_act_table_set(LN_EXP)
                    act.wait_ge(lru_v, half + 1)
                    own.did(act.activation(lv[:, :, :], lv[:, :, :], ACT.Ln, scale=1.0 / 16))
                    own.settle()
                    act.activation(lv[:, :, :], lv[:, :, :], ACT.Exp, scale=0.5).then_inc(lru_mult, 1)
                if n - 1 in YC_AT:
                    half = YC_AT.index(n - 1)
                    act.wait_ge(lru_h, half + 1)
                    act.activation(y0hi[:, 4 * half:4 * half + 4, :], G[:, 4 * half:4 * half + 4, :], ACT.Copy)\
                       .then_inc(yc_hi, 1)
                if n in LRU_AT:
                    split_at(n + RING)
                    i = LRU_AT.index(n)
                    act.wait_ge(lru_mm, i + 1)
                    if i > 0:
                        act.wait_ge(lru_p, i)
                    for t in range(2):
                        c = 2 * i + t
                        act.activation(thr[:, t, :], banks[:, 4 + 2 * t, 0:T], ACT.Tanh, scale=0.5,
                                       bias=ba2[:, c:c + 1])
                        ins = act.activation(thx[:, t, :], banks[:, 5 + 2 * t, 0:T], ACT.Tanh, scale=0.5,
                                             bias=bx2[:, c:c + 1])
                    ins.then_inc(lru_acted, 1)
                    act.wait_ge(lru_acted, i + 1)
                    if i == 2:
                        act.wait_ge(lru_scan, 1)
                    for t in range(2):
                        c = 2 * i + t
                        act.activation(la[:, c % 4, :], thr[:, t, :], ACT.Exp, scale=cpos[:, c:c + 1],
                                       bias=cpos[:, c:c + 1])
                        ins = act.activation(lv[:, c % 4, :], thr[:, t, :], ACT.Tanh, scale=cneg[:, c:c + 1],
                                             bias=cneg[:, c:c + 1])
                    ins.then_inc(lru_a, 1)
                if XBC + 1 <= n < XBC + 7:
                    i = n - XBC - 1
                    act.wait_ge(conv_done, 5 + i)
                    if i > 0:
                        act.wait_ge(xbc_ready, i)
                    else:
                        act.wait_ge(gate_done, 4)
                    act.activation(th[:, :, :], XT[:, 2 * i:2 * i + 2, :], ACT.Tanh, scale=0.5).then_inc(xbc_th, 1)
                if n == QQ - 2:
                    act.wait_ge(cb_mm, 1)
                    for g in range(2):
                        act.activation(CB[:, g, :], banks[:, 4 + 2 * g, 0:3 * P], ACT.Copy, scale=0.25)
                        ins = act.activation(CBA[:, g, :], banks[0:META, 5 + 2 * g, 0:2 * P], ACT.Copy, scale=0.25)
                    ins.then_inc(cb_done, 1)
                if QQ - 1 <= n < QQ + 7:
                    if n == QQ - 1:
                        act.wait_ge(tok_ready, 1)
                        act.preload_act_table_set(LN_EXP)
                    decay_exps(n - QQ + 1)
                if n in (QQ + 4, QQ + 8):
                    g = (n - QQ - 4) // 4
                    act.wait_ge(gstat, 4 * g + 4)
                    if g == 1:
                        act.wait_ge(yb_scaled, 1)
                    own.did(act.activation(acc[:, 0:TQ], banks[:, 7, 0:TQ], ACT.Ln, bias=eps[:, 0:1],
                                           scale=1.0 / (4 * P)))
                    own.settle()
                    act.activation(acc[:, 0:TQ], acc[:, 0:TQ], ACT.Exp, scale=-0.5).then_inc(grs_done, 1)
                if QQ <= n < QQ + 8:
                    c = n - QQ
                    if c > 0:
                        act.wait_ge(gstat, c)
                    act.wait_ge(y_evac, c + 1)
                    act.activation(ysq, Z[:, c, :], ACT.Square).then_inc(ysq_done, 1)
                if n in (QQ + 5, QQ + 9):
                    g = (n - QQ - 5) // 4
                    act.wait_ge(yb_scaled, g + 1)
                    act.activation(y1hi[:, 4 * g:4 * g + 4, :], Z[:, 4 * g:4 * g + 4, :], ACT.Copy).then_inc(yb_hi, 1)
                if VV <= n < MG:
                    i = n - VV
                    act.wait_ge(v_tr, i + 1)
                    act.wait_ge(y_evac, C)
                    act.activation(VM[:, :, 2 * P * i:2 * P * (i + 1)].rearrange("p j (c x) -> p c j x", c=2),
                                   banks[:, 4, :].rearrange("p (c j x) -> p c j x", c=2, j=2),
                                   ACT.Copy).then_inc(v_main, 1)
                if VV + 2 <= n < VV + 19:
                    h = n - VV - 2
                    if h == 0:
                        act.preload_act_table_set(EXP_TANH)
                    if h < H:
                        act.wait_ge(s_max, h + 1)
                        if h >= 2:
                            act.wait_ge(p_tr, h - 1)
                        act.activation(PR[:, h % 2, 0:144], banks[:, 6, 0:144], ACT.Exp,
                                       bias=NM[:, 2 * h:2 * h + 1], accum_out=RS[:, 2 * h:2 * h + 1])
                        act.activation(PR[:, h % 2, 144:416], banks[:, 6, 144:416], ACT.Exp,
                                       bias=NM[:, 2 * h + 1:2 * h + 2], accum_out=RS[:, 2 * h + 1:2 * h + 2])\
                           .then_inc(s_exp, 1)
                    if h >= 1:
                        act.wait_ge(p_tr, h)
                        if h >= 3:
                            act.wait_ge(av_mm, h - 2)
                        act.activation(PT[:, (h - 1) % 2, :], banks[:, 7, 0:3 * P], ACT.Copy).then_inc(pt_main, 1)
                if MG + 16 <= n < WO:
                    m = n - MG - 16
                    act.wait_ge(mix_new, m + 1)
                    act.activation(y1hi[:, m, :], MIX[:, m, :], ACT.Copy, scale=0.5).then_inc(mix_hi, 1)
                if WO <= n < GU2:
                    squares(2, n - WO, OUTS)

                if n not in LRU_AT and n < GU2 - 1:
                    split_at(n + RING)

            norm(2, OUTS)
            split_at(GU2 + 2)
            ffn(3, GU2, OUTS, FC)
            norm(3, OUTS)
            for half in range(2):
                act.wait_ge(o_tr, 4 * half + 4)
                act.activation(tokio[:, 1, 512 * half:512 * (half + 1)], banks[:, 2 * half + 1, :], ACT.Copy)\
                   .then_inc(o_act, 1)

        @block.vector
        def _(dve):
            own = Own(dve, dve_own)

            def split(n, slot, w):
                dve.wait_ge(hi_done, n + 1)
                dve.tensor_tensor(wlo[:, slot, 0:w], raw[:, slot, 0:w], whi[:, slot, 0:w].bitcast(F32), ALU.subtract)\
                   .then_inc(lo_done, 1)

            def split_at(n):
                if n < END:
                    split(n, n % RING, width(n))

            def norm(q, gain, cols):
                w = cols.stop - cols.start
                dve.wait_ge(rstd_done, q + 1)
                for c in range(C + 1):
                    if c < C:
                        if q == 3 and c >= RING:
                            dve.wait_ge(o_tr, c + 1 - RING)
                        elif c >= RING:
                            dve.wait_ge(act_ready, C * q + c + 1 - RING)
                        dve.scalar_tensor_tensor(hn[:, c % RING, 0:w], xres[:, c, cols], col(gain, c), rstd[:, cols],
                                                 ALU.mult, ALU.mult).then_inc(hn_done, 1)
                    if c > 0 and q < 3:
                        dve.wait_ge(nhi_done, C * q + c)
                        dve.tensor_tensor(tlo[:, c - 1, cols], hn[:, (c - 1) % RING, 0:w],
                                          thi[:, c - 1, cols].bitcast(F32), ALU.subtract).then_inc(act_ready, 1)

            dve.memset(eps[:, :], EPS).then_inc(eps_set, 1)
            dve.memset(scl48[:, :], 0.0).then_inc(scl_zero, 1)
            for c in range(C):
                dve.wait_ge(xt_done, c + 1)
                dve.tensor_copy(xres[:, c, :], banks[:, c % 6, 0:T]).then_inc(x_new, 1)
            dve.wait_ge(vt_done, 1)
            dve.tensor_copy(colA[:, 0:nA], banks[:, 6, 0:nA]).then_inc(cols_done, 1)
            dve.tensor_copy(colB[:, 0:nB], banks[:, 6, P:P + nB]).then_inc(cols_done, 1)
            dve.wait_ge(cols_done, 2)
            split_at(0)
            norm(0, "ffn1_norm", ALL)
            for n in range(1, RING):
                split_at(n)

            dve.wait_ge(lam_act, 1)
            dve.tensor_scalar(cpos, lam_e, 1.0, None, ALU.add).then_inc(lam_dve, 1)
            own.did(dve.tensor_scalar(ba2, colB[:, cB["lru_b_a"]:cB["lru_b_a"] + 8], 0.5, None, ALU.mult))
            own.did(dve.tensor_scalar(bx2, colB[:, cB["lru_b_x"]:cB["lru_b_x"] + 8], 0.5, None, ALU.mult))
            dve.wait_ge(lam_act, 3)
            own.did(dve.tensor_scalar(cneg, cpos, 1.0, 1e-10, ALU.subtract, ALU.max))
            own.did(dve.tensor_scalar(lam_l, lam_l, 1e-10, None, ALU.max))
            own.settle()
            own.did(dve.reciprocal(cneg, cneg))
            own.did(dve.tensor_tensor(lam_l, lam_l, lam_e, ALU.mult))
            own.settle()
            own.did(dve.tensor_tensor(lam_l, lam_l, cneg, ALU.mult))
            own.did(dve.tensor_scalar(lam_e, lam, -1.0, 0.0, ALU.mult, ALU.max))
            own.settle()
            own.did(dve.tensor_tensor(lam_l, lam_l, lam_e, ALU.add))
            own.settle()
            own.did(dve.tensor_scalar(cpos, lam_l, -4.0, None, ALU.mult))
            own.did(dve.tensor_scalar(cneg, lam_l, 4.0, None, ALU.mult))
            dve.wait_ge(sml_in, 80)
            own.did(dve.tensor_scalar(dcol[:, :], dcol[:, :], 0.25, None, ALU.mult))
            own.did(dve.tensor_scalar(scl48[0:H, 0:1], scl48[0:H, 0:1], -1.0, None, ALU.mult))
            own.did(dve.memset(scl48[0:H, 1:2], -1.0))
            own.did(dve.memset(scl48[32:48, 1:2], 1.0))
            own.did(dve.memset(scl48[0:H, 3:4], 1.0))
            own.settle()
            dve.tensor_scalar(scl48[32:48, 3:4], scl48[32:48, 3:4], -1.0, None, ALU.mult).then_inc(scl_ready, 1)

            def ffn(q, first, cols, base):
                w = cols.stop - cols.start

                def one(t, m):
                    return t[:, m:m + 1, cols] if isinstance(m, int) else t[:, bass.ds(m, 1), cols]

                def gate_up(n, slot, arr, turn, j, wide=SLAB):
                    m = n - first
                    dve.wait_ge(silu_done, m + (base + 1))
                    dve.wait_ge(tiles_done, 2 * n + 2)
                    dve.tensor_tensor(hn[:, slot, 0:w], stmp[:, slot, 0:w], banks[:, 2 * slot + 1, 0:w], ALU.mult)\
                       .then_inc(h_done, 1)
                    split(n + RING, slot, wide)
                    dve.wait_ge(hhi_done, m + (base + 1))
                    dve.tensor_tensor(one(hid_lo, m), hn[:, slot:slot + 1, 0:w], one(hid_hi, m).bitcast(F32),
                                      ALU.subtract).then_inc(hlo_done, 1)

                rounds(dve, first, FC - RING, gate_up)
                for n in range(first + FC - RING, first + FC):
                    gate_up(n, n % RING, 0, 0, 0, wide=width(n + RING))

                def down(n, slot, arr, turn, j, ahead=True):
                    if j == 2:
                        for t in range(2):
                            dve.wait_ge(tiles_done, 2 * n + (1 + t))
                            x = one(xres, turn * 2 + t)
                            dve.scalar_tensor_tensor(x, banks[:, 2 + t:3 + t, 0:w], 0.5, x, ALU.mult, ALU.add)\
                               .then_inc(x_new, 1)
                        if ahead:
                            split(n + RING - 1, (slot - 1) % RING, SLAB)
                    if ahead and j != 1:
                        split(n + RING, slot, (FC - 16) * 2 * P if j == 2 else SLAB)

                d0 = first + FC
                rounds(dve, d0, 9, down)
                for j in range(RING):
                    down(d0 + 9 + j, (d0 + 9 + j) % RING, 0, 3, j, ahead=False)
                    if j == 0:
                        split_at(d0 + 12)

            ffn(1, GU1, ALL, 0)
            norm(1, "mix_norm", ALL)
            own.did(dve.memset(craw[:, :, :, 0:3], 0.0))
            split_at(FIRST + 1)
            split_at(FIRST + 2)
            own.settle()

            def conv(n, i, name_w, c0, dest, stride):
                dve.wait_ge(evac[n % 2], freed(n))
                for k in (2, 1, 0):
                    for t in range(2):
                        ins = dve.scalar_tensor_tensor(dest[:, c0 + t, :], craw[:, i % 2, t, k:k + T],
                                                       col(name_w, k * stride + c0 + t), dest[:, c0 + t, :],
                                                       ALU.mult, ALU.add)
                        if k > 0:
                            own.did(ins)
                    if k > 0:
                        own.settle()
                ins.then_inc(conv_done, 1)

            for n in range(FIRST, GU2):
                if ZZ <= n < QQ:
                    j = n - ZZ
                    dve.wait_ge(z_th, j + 1)
                    zp = Z[:, 2 * j:2 * j + 2, :]
                    dve.scalar_tensor_tensor(zp, zp, 1.0, banks[:, pj(n):pj(n) + 2, 0:TQ], ALU.add, ALU.mult)\
                       .then_inc(evac[n % 2], 1)
                elif MG <= n < WO:
                    k = n - MG
                    m = k % C
                    dve.wait_ge(mg_th, k + 1)
                    dve.wait_ge(tiles_done, 2 * n + 2)
                    dst = MIX[:, m, :] if k < C else hn[:, 2, 0:TQ]
                    if C < k <= 2 * C:
                        own.settle()
                    elif k > 2 * C:
                        dve.wait_ge(mix_new, k - 2 * C)
                    dve.scalar_tensor_tensor(dst, mt[:, k % 2, 0:TQ], 1.0, banks[:, pj(n) + 1, 0:TQ],
                                             ALU.add, ALU.mult).then_inc(evac[n % 2], 1)
                    if k >= C:
                        dve.wait_ge(evac[n % 2], freed(n))
                        ins = dve.tensor_tensor(MIX[:, m, :], MIX[:, m, :], dst, ALU.add)
                        if k >= 2 * C:
                            ins.then_inc(mix_new, 1)
                        else:
                            own.did(ins)
                elif n >= WO:
                    for t in range(2):
                        c = 2 * (n - WO) + t
                        dve.wait_ge(tiles_done, 2 * n + 1 + t)
                        dve.tensor_tensor(xres[:, c, OUTS], xres[:, c, OUTS], banks[:, pj(n) + t, 0:TQ], ALU.add)\
                           .then_inc(x_new, 1)

                if n in YT_AT and YT_AT[n] < 3:
                    attn_lo(dve, YT_AT[n])
                if n == FDT:
                    dve.wait_ge(fdt_act, 1)
                    dve.tensor_scalar(u48, e48, 1.0, None, ALU.add).then_inc(fdt_dve, 1)
                    own.did(dve.memset(one48, 1.0))
                    dve.wait_ge(fdt_act, 2)
                    own.did(dve.tensor_scalar(u48, u48, 1.0, 1e-10, ALU.subtract, ALU.max))
                    own.did(dve.tensor_scalar(l48, l48, 1e-10, None, ALU.max))
                    own.settle()
                    own.did(dve.reciprocal(u48, u48))
                    own.did(dve.tensor_tensor(l48, l48, e48, ALU.mult))
                    own.settle()
                    own.did(dve.tensor_tensor(l48, l48, u48, ALU.mult))
                    own.settle()
                    own.did(dve.scalar_tensor_tensor(sp48, xt48, 0.0, l48, ALU.max, ALU.add))
                    own.settle()
                    own.did(dve.tensor_scalar(e48, sp48, scl48[:, 3:4], None, ALU.mult))
                    own.settle()
                    dve.tensor_tensor_scan(cs48, one48, e48, 0.0, ALU.mult, ALU.add).then_inc(fdt_dve, 1)
                if n == FDT + 2:
                    dve.wait_ge(fdt_tr, 1)
                    dve.tensor_scalar(tokm[:, 0:96], banks[:, 7, 0:96], 0.25, None, ALU.mult)
                    dve.tensor_scalar(tokm[:, 96:192], banks[:, 7, 96:192], -1.0, None, ALU.mult)
                    dve.tensor_scalar(toka[:, 0:48], banks[0:META, 7, 192:240], 0.25, None, ALU.mult)
                    dve.tensor_scalar(toka[:, 48:96], banks[0:META, 7, 240:288], -1.0, None, ALU.mult)\
                       .then_inc(tok_ready, 1)
                    dve.wait_ge(cs_rounded, 1)
                    dve.tensor_tensor(cs_lo[:, :], cs48, cs_hi[:, :].bitcast(F32), ALU.subtract).then_inc(cs_split, 1)
                if n in XR:
                    conv(n, XR.index(n), "lru_conv_w", 2 * XR.index(n), XC, C)
                if n in GATE:
                    j = GATE.index(n)
                    gp, tp = G[:, 2 * j:2 * j + 2, :], th[:, :, 0:TQ]
                    dve.wait_ge(evac[n % 2], freed(n))
                    dve.scalar_tensor_tensor(tp, tp, 1.0, gp, ALU.add, ALU.mult).then_inc(gate_arg, 1)
                    dve.wait_ge(gate_th, j + 1)
                    dve.scalar_tensor_tensor(gp, tp, 1.0, gp, ALU.add, ALU.mult).then_inc(gate_done, 1)
                if n in SCAN_AT:
                    half = SCAN_AT.index(n)
                    hs = slice(4 * half, 4 * half + 4)
                    dve.wait_ge(lru_mult, half + 1)
                    own.did(dve.tensor_tensor(lv[:, :, :], lv[:, :, :], XC[:, hs, :], ALU.mult))
                    own.settle()
                    for c in range(4):
                        ins = dve.tensor_tensor_scan(XC[:, 4 * half + c, :], la[:, c, :], lv[:, c, :], 0.0,
                                                     ALU.mult, ALU.add)
                    ins.then_inc(lru_scan, 1)
                if n in YC_AT:
                    half = YC_AT.index(n)
                    hs = slice(4 * half, 4 * half + 4)
                    dve.wait_ge(lru_scan, half + 1)
                    dve.wait_ge(gate_done, 2 * half + 2)
                    dve.tensor_tensor(G[:, hs, :], XC[:, hs, OUTS], G[:, hs, :], ALU.mult).then_inc(lru_h, 1)
                if n - 1 in YC_AT:
                    half = YC_AT.index(n - 1)
                    hs = slice(4 * half, 4 * half + 4)
                    dve.wait_ge(yc_hi, half + 1)
                    dve.tensor_tensor(y0lo[:, hs, :], G[:, hs, :], y0hi[:, hs, :].bitcast(F32), ALU.subtract)\
                       .then_inc(yc_ready, 1)
                if n in LRU_AT:
                    split_at(n + RING)
                    i = LRU_AT.index(n)
                    dve.wait_ge(lru_a, i + 1)
                    for t in range(2):
                        c = 2 * i + t
                        own.did(dve.scalar_tensor_tensor(XC[:, c, :], thx[:, t, :], 1.0, XC[:, c, :],
                                                         ALU.add, ALU.mult))
                        own.did(dve.tensor_tensor(thr[:, t, :], la[:, c % 4, :], la[:, c % 4, :], ALU.mult))
                    own.settle()
                    for t in range(2):
                        c = 2 * i + t
                        ins = dve.scalar_tensor_tensor(lv[:, c % 4, :], thr[:, t, :], 1.0, lv[:, c % 4, :],
                                                       ALU.add, ALU.mult)
                    ins.then_inc(lru_p, 1)
                    if i % 2:
                        dve.wait_ge(lru_p, i + 1)
                        own.did(dve.tensor_scalar(lv[:, :, :], lv[:, :, :], 1e-16, None, ALU.max))
                        own.settle()
                        dve.memset(lv[:, :, 0:1], 1.0).then_inc(lru_v, 1)
                if XBC <= n < ZZ:
                    conv(n, 4 + n - XBC, "ssd_conv_w", 2 * (n - XBC), XT, 12)
                if XBC + 1 <= n < XBC + 7:
                    i = n - XBC - 1
                    dve.wait_ge(xbc_th, i + 1)
                    xp = XT[:, 2 * i:2 * i + 2, :]
                    dve.scalar_tensor_tensor(xp, th[:, :, :], 1.0, xp, ALU.add, ALU.mult).then_inc(xbc_ready, 1)
                if XBC + 3 <= n < XBC + 7:
                    p = n - XBC - 3
                    if p == 0:
                        dve.wait_ge(tok_ready, 1)
                    dve.wait_ge(x_tr, p + 1)
                    for c in range(2):
                        o = 2 * P * p + P * c
                        h0 = 32 + 4 * p + 2 * c
                        dt = tokm[:, 0:96].rearrange("p (j k) -> p j k", j=2)[:, :, h0:h0 + 2]
                        dve.tensor_tensor(XDM[:, :, o:o + P].rearrange("p j (h x) -> p j h x", h=2),
                                          banks[:, 4, 2 * P * c:2 * P * (c + 1)]
                                          .rearrange("p (j h x) -> p j h x", j=2, h=2),
                                          dt.unsqueeze(3).broadcast_to([P, 2, 2, DH]), ALU.mult)
                    dve.tensor_tensor(XDA[:, 2 * P * p:2 * P * (p + 1)].rearrange("p (h x) -> p h x", h=4),
                                      banks[0:META, 5, 0:2 * P].rearrange("p (h x) -> p h x", h=4),
                                      toka[:, 32 + 4 * p:36 + 4 * p].unsqueeze(2).broadcast_to([META, 4, DH]),
                                      ALU.mult).then_inc(xdt_done, 1)
                if QQ - 1 <= n < QQ + 7:
                    i = n - QQ + 1
                    g = i // 4
                    if i == 0:
                        dve.wait_ge(cb_done, 1)
                    for b in range(2):
                        dve.wait_ge(dec_exp, 2 * i + b + 1)
                        dve.tensor_tensor(E[:, b, :], E[:, b, :], CB[:, g, :], ALU.mult)
                        dve.tensor_tensor(EA[:, b, :], EA[:, b, :], CBA[:, g, :], ALU.mult).then_inc(w_done, 1)
                if QQ <= n < QQ + 8:
                    c = n - QQ
                    dve.wait_ge(y_done, c + 1)
                    own.did(dve.scalar_tensor_tensor(ytmp, XT[:, c, OUTS], dcol[:, c:c + 1], banks[:, 6, 0:TQ],
                                                     ALU.mult, ALU.add))
                    own.settle()
                    dve.tensor_tensor(Z[:, c, :], Z[:, c, :], ytmp, ALU.mult).then_inc(y_evac, 1)
                if n in (QQ + 5, QQ + 9):
                    g = (n - QQ - 5) // 4
                    dve.wait_ge(yb_hi, g + 1)
                    dve.tensor_tensor(y1lo[:, 4 * g:4 * g + 4, :], Z[:, 4 * g:4 * g + 4, :],
                                      y1hi[:, 4 * g:4 * g + 4, :].bitcast(F32), ALU.subtract).then_inc(yb_ready, 1)
                if n in (QQ + 4, QQ + 8):
                    g = (n - QQ - 4) // 4
                    dve.wait_ge(grs_done, g + 1)
                    for c in range(4 * g, 4 * g + 4):
                        ins = dve.scalar_tensor_tensor(Z[:, c, :], Z[:, c, :], col("ssd_norm", c), acc[:, 0:TQ],
                                                       ALU.mult, ALU.mult)
                    ins.then_inc(yb_scaled, 1)
                if VV <= n < MG:
                    i = n - VV
                    dve.wait_ge(v_tr, i + 1)
                    dve.tensor_copy(VA[:, 2 * P * i:2 * P * (i + 1)], banks[0:META, 5, 0:2 * P]).then_inc(v_meta, 1)
                if VV + 2 <= n < VV + 19:
                    h = n - VV - 2
                    if h < H:
                        dve.wait_ge(s_mm, h + 1)
                        dve.reduce_max(NM[:, 2 * h:2 * h + 1], banks[:, 6, 0:144], AX_X, negate=True)
                        dve.reduce_max(NM[:, 2 * h + 1:2 * h + 2], banks[:, 6, 144:416], AX_X, negate=True)\
                           .then_inc(s_max, 1)
                    if h >= 1:
                        dve.wait_ge(p_tr, h)
                        if h >= 3:
                            dve.wait_ge(av_mm, h - 2)
                        dve.tensor_copy(PTA[:, (h - 1) % 2, :], banks[0:META, 5, 0:2 * P]).then_inc(pt_meta, 1)
                if n >= VV + 7 and (n - VV - 7) % 4 == 0 and (n - VV - 7) // 4 < 4:
                    g = (n - VV - 7) // 4
                    dve.wait_ge(av_mm, 4 * g + 4)
                    own.did(dve.reciprocal(RI[:, 8 * g:8 * g + 8], RS[:, 8 * g:8 * g + 8]))
                    own.settle()
                    dve.tensor_tensor(YTOK[:, :, 2 * P * g:2 * P * (g + 1)].rearrange("p j (h x) -> p h j x", h=4),
                                      banks[:, 4, :].rearrange("p (h j x) -> p h j x", h=4, j=2),
                                      RI[:, 8 * g:8 * g + 8].rearrange("p (h j) -> p h j", h=4).unsqueeze(3)
                                      .broadcast_to([P, 4, 2, DH]), ALU.mult).then_inc(ytok_done, 1)
                if n in YT_AT and YT_AT[n] == 3:
                    attn_lo(dve, 3)
                if MG + 16 <= n < WO:
                    m = n - MG - 16
                    dve.wait_ge(mix_hi, m + 1)
                    dve.scalar_tensor_tensor(y1lo[:, m, :], MIX[:, m, :], 0.5, y1hi[:, m, :].bitcast(F32),
                                             ALU.mult, ALU.subtract).then_inc(mix_ready, 1)

                if n not in LRU_AT and n < GU2 - 1:
                    split_at(n + RING)

            norm(2, "ffn2_norm", OUTS)
            split_at(GU2 + 2)
            ffn(3, GU2, OUTS, FC)
            norm(3, "final_norm", OUTS)
            for half in range(2):
                dve.wait_ge(o_tr, 4 * half + 4)
                dve.tensor_copy(tokio[:, 0, 512 * half:512 * (half + 1)], banks[:, 2 * half, :]).then_inc(o_dve, 1)

        @block.tensor
        def _(pe):
            def product(bank_out, slot, kcs, tile, rhs, cols, start, stop, ready=None):
                for k in range(kcs):
                    if ready is not None:
                        pe.wait_ge(ready[0], ready[1] + k + 1)
                    o = (2 * k + tile) * P
                    for i, (w, x) in enumerate(((whi, 0), (whi, 1), (wlo, 0))):
                        last = pe.matmul(bank_out, w[:, slot, o:o + P], rhs[x][:, rhs[2] + k, cols],
                                         start=start and k == 0 and i == 0, stop=stop and k == kcs - 1 and i == 2)
                return last

            def pair(n, slot, bank, cols, done):
                w = cols.stop - cols.start
                for k in range(KC):
                    pe.wait_ge(act_ready, done + k + 1)
                    for t in range(2):
                        o = (2 * k + t) * P
                        for i, (wt, x) in enumerate(((whi, thi), (whi, tlo), (wlo, thi))):
                            last = pe.matmul(banks[:, bank + t, 0:w], wt[:, slot, o:o + P], x[:, k, cols],
                                             start=k == 0 and i == 0, stop=k == KC - 1 and i == 2)
                        if k == KC - 1:
                            last.then_inc(tiles_done, 1)

            def stats(q, cols):
                w = cols.stop - cols.start
                pe.wait_ge(sq_sum, q + 1)
                pe.matmul(banks[:, 7, 0:w], ones[:, :], acc[:, cols], start=True, stop=False)
                pe.wait_ge(sq_done, 4 * q + 4)
                pe.matmul(banks[:, 7, 0:w], ones[:, :], sq[:, C - 2, cols], start=False, stop=False)
                pe.matmul(banks[:, 7, 0:w], ones[:, :], sq[:, C - 1, cols], start=False, stop=True)\
                  .then_inc(stat_done, 1)

            NRM = (thi, tlo, 0)
            Y0 = (y0hi, y0lo, 0)
            Y1 = (y1hi, y1lo, 0)

            pe.wait_ge(consts, 4)
            pe.wait_ge(x_in, 32)
            for c in range(C):
                if c >= 6:
                    pe.wait_ge(x_new, c - 5)
                pe.transpose(banks[:, c % 6, 0:META], metain[:, P * c:P * (c + 1)], ident[0:META, 0:META])
                for j in range(2):
                    last = pe.transpose(banks[:, c % 6, META + P * j:META + P * (j + 1)],
                                        tokio[:, j, P * c:P * (c + 1)], ident[:, :])
                last.then_inc(xt_done, 1)
            pe.wait_ge(vec_in, 16 * 12)
            pe.transpose(banks[:, 6, 0:nA], rows[0:nA, 0, :], ident[0:nA, 0:nA])
            pe.transpose(banks[:, 6, P:P + nB], rows[0:nB, 1, :], ident[0:nB, 0:nB]).then_inc(vt_done, 1)
            stats(0, ALL)

            def ffn(q, first, cols, base):
                w = cols.stop - cols.start

                def gate_up(n, slot, arr, turn, j, ready=None):
                    pe.wait_ge(lo_done, n + 1)
                    if base > 0 or not (isinstance(n, int) and n < first + RING):
                        pe.wait_ge(h_done, n + (base - first - RING + 1))
                    if ready is not None:
                        pair(n, slot, 2 * slot, cols, ready)
                        return
                    for t in range(2):
                        product(banks[:, 2 * slot + t, 0:w], slot, KC, t, NRM, cols, True, True)\
                            .then_inc(tiles_done, 1)

                peel = RING if base == 0 else 1
                for n in range(first, first + peel):
                    gate_up(n, n % RING, 0, 0, 0, C * (q - 1) if n == first else None)
                rounds(pe, first + peel, FC - peel, gate_up)

                d0 = first + FC

                def down(n, slot, arr, turn, j):
                    kcs = FC - 16 if j == 2 else KC
                    pe.wait_ge(lo_done, n + 1)
                    if isinstance(n, int) and n < d0 + RING:
                        pe.wait_ge(hlo_done, base + 8 * j + kcs)
                        pe.wait_ge(h_done, base + FC - 2)
                    for t in range(2):
                        if j == 0 and not (isinstance(n, int) and n < d0 + RING):
                            pe.wait_ge(x_new, turn * 2 + (C * q + 1 + t))
                        product(banks[:, 2 + t, 0:w], slot, kcs, t, (hid_hi, hid_lo, 8 * j), cols,
                                j == 0, j == 2).then_inc(tiles_done, 1)

                for j in range(RING):
                    down(d0 + j, (d0 + j) % RING, 0, 0, j)
                rounds(pe, d0 + RING, 9, down)
                stats(q, cols)

            ffn(1, GU1, ALL, 0)

            def head(h):
                return slice(DH * (h % 2), DH * (h % 2) + DH), h // 2

            for n in range(FIRST, GU2):
                slot = n % RING
                pe.wait_ge(lo_done, n + 1)
                if FIRST + 2 <= n < WO + 2:
                    pe.wait_ge(evac[n % 2], freed(n - 2))
                elif n >= WO + 2:
                    pe.wait_ge(x_new, 2 * C + 2 * (n - WO - 2) + 2)
                cols = OUTS if n in GATE or ZZ <= n < KK or n >= MG else ALL
                w = cols.stop - cols.start
                if n == FIRST:
                    pair(n, slot, pj(n), cols, C)
                elif n == FDT:
                    product(banks[:, pj(n), 0:w], slot, KC, 0, NRM, cols, True, True).then_inc(tiles_done, 2)
                elif n < MG:
                    for t in range(2):
                        product(banks[:, pj(n) + t, 0:w], slot, KC, t, NRM, cols, True, True)\
                            .then_inc(tiles_done, 1)
                elif n < WO:
                    product(banks[:, pj(n), 0:w], slot, KC, 0, NRM, cols, True, True).then_inc(tiles_done, 1)
                    k = n - MG
                    if k == 0:
                        pe.wait_ge(yc_ready, 2)
                    if k == C:
                        pe.wait_ge(yb_ready, 2)
                    if k == 2 * C:
                        pe.wait_ge(ya_ready, 4)
                    product(banks[:, pj(n) + 1, 0:w], slot, KC, 1, Y1 if C <= k < 2 * C else Y0, slice(0, TQ),
                            True, True).then_inc(tiles_done, 1)
                else:
                    for t in range(2):
                        product(banks[:, pj(n) + t, 0:w], slot, KC, t, Y1, slice(0, TQ), True, True,
                                (mix_ready, 0) if n == WO and t == 0 else None).then_inc(tiles_done, 1)

                if n in YT_AT and YT_AT[n] < 3:
                    attn_turn(pe, YT_AT[n], n - VV - 3)
                if n == FDT + 2:
                    pe.wait_ge(fdt_dve, 2)
                    pe.wait_ge(lru_acted, 4)
                    for src, o, oa in ((sp48, 0, 192), (cs48, 96, 240)):
                        for j, ts in enumerate((T0, T1)):
                            pe.transpose(banks[:, 7, o + 48 * j:o + 48 * (j + 1)], src[:, ts], ident[0:48, 0:48])
                        last = pe.transpose(banks[0:META, 7, oa:oa + 48], src[:, 0:META], ident[0:48, 0:48])
                    last.then_inc(fdt_tr, 1)
                if n in LRU_AT:
                    i = LRU_AT.index(n)
                    pe.wait_ge(conv_done, i + 1)
                    if i == 0:
                        pe.wait_ge(lru_w_in, 64)
                    else:
                        pe.wait_ge(lru_acted, i)
                    for t in range(2):
                        c = 2 * i + t
                        pe.matmul(banks[:, 4 + 2 * t, 0:T], bda[:, c, :], XC[:, c, :], start=True, stop=True)
                        last = pe.matmul(banks[:, 5 + 2 * t, 0:T], bdx[:, c, :], XC[:, c, :], start=True, stop=True)
                    last.then_inc(lru_mm, 1)
                if XBC + 3 <= n < XBC + 7:
                    p = n - XBC - 3
                    pe.wait_ge(xbc_ready, p + 1)
                    if p == 0:
                        pe.wait_ge(lru_acted, 4)
                    else:
                        pe.wait_ge(xdt_done, p)
                    last = to_tokens(pe, lambda c, ts: XT[:, 2 * p + c, ts])
                    last.then_inc(x_tr, 1)
                if n == QQ - 2:
                    pe.wait_ge(xbc_ready, 6)
                    pe.wait_ge(xdt_done, 4)
                    for g in range(2):
                        B, Cm = XT[:, 8 + g, :], XT[:, 10 + g, :]
                        pe.matmul(banks[:, 4 + 2 * g, 0:2 * P], B[:, T0], Cm[:, OUTS], start=True, stop=True)
                        pe.matmul(banks[:, 4 + 2 * g, 2 * P:3 * P], B[:, T1], Cm[:, T1], start=True, stop=True)
                        pe.matmul(banks[0:META, 5 + 2 * g, 0:P], B[:, 0:META], Cm[:, T1], start=True, stop=True)
                        last = pe.matmul(banks[0:META, 5 + 2 * g, P:2 * P], B[:, 0:META], Cm[:, T0],
                                         start=True, stop=True)
                    last.then_inc(cb_mm, 1)
                if QQ - 1 <= n < QQ + 7:
                    i = n - QQ + 1
                    if i == 0:
                        pe.wait_ge(cb_done, 1)
                        pe.wait_ge(cs_split, 1)
                        pe.wait_ge(sel_done, 1)
                    else:
                        pe.wait_ge(dec_exp, 2 * i)
                    for b in range(2):
                        h = 2 * i + b
                        row = 32 + h
                        for part in (cs_hi, cs_lo):
                            pe.matmul(banks[:, 4 + b, :].rearrange("p (r t) -> p r t", r=2),
                                      sel[32:48, row:row + 1].broadcast_to([H, P]), part[32:48, OUTS].unsqueeze(1).broadcast_to([H, 2, TQ]),
                                      start=part is cs_hi, stop=False)
                        pe.matmul(banks[:, 4 + b, 0:P], identb[:, :], mask_st[:, :], start=False, stop=False)
                        pe.matmul(banks[:, 4 + b, 3 * P:4 * P], identb[:, :], mask_st[:, :], start=False, stop=True)\
                          .then_inc(dec_mm, 1)
                if QQ <= n < QQ + 8:
                    i = n - QQ
                    pe.wait_ge(w_done, 2 * i + 2)
                    if i > 0:
                        pe.wait_ge(y_evac, i)
                    for b in range(2):
                        h = 2 * i + b
                        hs = slice(DH * h, DH * (h + 1))
                        y = banks[DH * b:DH * (b + 1), 6, :]
                        pe.matmul(y[:, 0:2 * P], XDM[:, 0, hs], E[:, b, 0:2 * P], start=True, stop=False)
                        pe.matmul(y[:, P:2 * P], XDM[:, 1, hs], E[:, b, 2 * P:3 * P], start=False, stop=False)
                        pe.matmul(y[:, P:2 * P], XDA[:, hs], EA[:, b, 0:P], start=False, stop=False)
                        last = pe.matmul(y[:, 0:P], XDA[:, hs], EA[:, b, P:2 * P], start=False, stop=True)
                    last.then_inc(y_done, 1)
                if QQ + 1 <= n < QQ + 9:
                    c = n - QQ - 1
                    pe.wait_ge(ysq_done, c + 1)
                    if c == 4:
                        pe.wait_ge(grs_done, 1)
                    pe.matmul(banks[:, 7, 0:TQ], ones[:, :], ysq, start=c % 4 == 0, stop=c % 4 == 3)\
                      .then_inc(gstat, 1)
                if VV <= n < MG:
                    i = n - VV
                    pe.wait_ge(evac[n % 2], freed(n))
                    if i == 0:
                        pe.wait_ge(dec_exp, H)
                    else:
                        pe.wait_ge(v_main, i)
                        pe.wait_ge(v_meta, i)
                    to_tokens(pe, lambda c, ts: th[:, c, ts]).then_inc(v_tr, 1)
                if VV + 2 <= n < VV + 20:
                    h = n - VV - 2
                    if h < H:
                        ps, c = head(h)
                        if h == 0:
                            pe.wait_ge(y_evac, C)
                        else:
                            pe.wait_ge(s_exp, h)
                        for o, e, q0, d in ((0, 144, 0, 16), (144, T, P, 288)):
                            s = banks[:, 6, o:o + e]
                            pe.matmul(s, QT[ps, c, q0:q0 + P], KT[ps, c, 0:e], start=o == 0, stop=False)
                            for part in (cs_hi, cs_lo):
                                pe.matmul(s, sel[0:H, h:h + 1].broadcast_to([H, P]), part[0:H, 0:e], start=False, stop=False)
                            last = pe.matmul(banks[:, 6, d:d + P], identb[:, :], mask_qk[:, :], start=False,
                                             stop=o > 0)
                        last.then_inc(s_mm, 1)
                    if h >= 2:
                        attn_values(pe, h - 2)
                    if 1 <= h <= H:
                        k = h - 1
                        pe.wait_ge(s_exp, h)
                        if k == 0:
                            pe.wait_ge(grs_done, 2)
                            pe.wait_ge(v_meta, 4)
                        else:
                            pe.wait_ge(pt_main, k)
                            pe.wait_ge(pt_meta, k)
                        turned = sum(1 for m in YT_AT if m <= n)
                        if turned:
                            pe.wait_ge(ya_ready, turned)
                        pr = PR[:, k % 2, :]
                        pe.transpose(banks[0:META, 5, 0:P], pr[:, 0:16], ident[:, :])
                        pe.transpose(banks[0:META, 5, P:2 * P], pr[:, 144:160], ident[:, :])
                        pe.transpose(banks[:, 7, 0:P], pr[:, 16:144], ident[:, :])
                        pe.transpose(banks[:, 7, P:2 * P], pr[:, 160:288], ident[:, :])
                        pe.transpose(banks[:, 7, 2 * P:3 * P], pr[:, 288:416], ident[:, :]).then_inc(p_tr, 1)
                if n in YT_AT and YT_AT[n] == 3:
                    attn_turn(pe, 3, H)

            stats(2, OUTS)
            ffn(3, GU2, OUTS, FC)
            for c in range(C):
                pe.wait_ge(hn_done, 3 * C + c + 1)
                for j in range(2):
                    last = pe.transpose(banks[:, 2 * (c // 4) + j, P * (c % 4):P * (c % 4 + 1)],
                                        hn[:, c % RING, P * j:P * (j + 1)], ident[:, :])
                last.then_inc(o_tr, 1)


_OUT = "out_dram"


def kernel(**inputs):
    import numpy as _np
    import concourse.bacc as _bacc
    from concourse import mybir as _mybir
    from concourse.bass_utils import run_bass_kernel_spmd as _run

    nc = _bacc.Bacc("TRN2", target_bir_lowering=False, num_devices=1)
    arrays, aps = {}, {}
    for name, value in inputs.items():
        v = _np.ascontiguousarray(value)
        arrays[f"in_{name}"] = v
        aps[name] = nc.dram_tensor(f"in_{name}", v.shape, _mybir.dt.from_np(v.dtype), kind="ExternalInput").ap()
    shape = tuple(inputs["x"].shape)
    out = nc.dram_tensor(_OUT, shape, _mybir.dt.float32, kind="ExternalOutput").ap()
    hybrid_trunk(nc, aps, out)
    r = _run(nc, [arrays], core_ids=[0])
    return r.results[0][_OUT]
```

```python
from contextlib import ExitStack

import numpy as np

import concourse.bass as bass
from concourse import mybir

F32 = mybir.dt.float32
F32R = mybir.dt.float32r
BF16 = mybir.dt.bfloat16
ALU = mybir.AluOpType
ACT = mybir.ActivationFunctionType
AX_X = mybir.AxisListType.X

P = 128
RING = 3
WARM = 8
KC = 8
SLAB = KC * 2 * P
NEG = -1.0e30
GELU_C = 0.044715
GELU_S = float(np.sqrt(2.0 / np.pi))
EPS = 1e-6
LN_EXP = "natural_log_exp_and_others"
EXP_TANH = "exp_and_others"


class Own:

    def __init__(self, eng, sem):
        self.eng, self.sem, self.n = eng, sem, 0

    def did(self, ins):
        ins.then_inc(self.sem, 1)
        self.n += 1
        return self.n

    def settle(self, n=None):
        self.eng.wait_ge(self.sem, self.n if n is None else n)


def hybrid_trunk(nc, a, out):
    D = a["x"].shape[2]
    SEQ = a["x"].shape[1]
    META = a["meta_tokens"].shape[0]
    T = META + SEQ
    TQ = SEQ
    DFF = a["ffn1_w_down"].shape[1]
    C = D // P
    FC = DFF // P
    H = a["ssd_d"].shape[1]
    DH = D // H
    assert (D, SEQ, META, H, DH, FC) == (1024, 256, 16, 16, 64, 22)
    ALL = slice(0, T)
    OUTS = slice(META, T)
    T0 = slice(META, META + P)
    T1 = slice(META + P, T)
    S0, S1, S2 = slice(0, P), slice(P, 2 * P), slice(2 * P, T)
    W1 = T - P
    W01 = TQ + W1

    w_in = a["w_in"][0]
    sizes = [D, D, D, H, D, D + 2 * 2 * P, H, D, D, 3 * D]
    starts = [int(v) for v in np.cumsum([0] + sizes)]
    oq, ok, ov, of, oz, oxbc, odt, oxr, ogate, omerge = starts[:10]

    GU1 = 0
    DN1 = GU1 + FC
    FIRST = DN1 + 12
    XR = [FIRST, FIRST + 2, FIRST + 4, FIRST + 6]
    FDT = FIRST + 1
    GATE = [FIRST + 3, FIRST + 5, FIRST + 7, FIRST + 8]
    XBC = [GATE[3] + k for k in (1, 3, 4, 6, 7, 8)]
    ZZ = [GATE[3] + k for k in (2, 5, 9, 10)]
    XBC_PAIR = dict(zip(XBC, (4, 5, 0, 1, 2, 3)))
    LRU_AT = [n + 2 for n in XR]
    KK = ZZ[3] + 1
    QQ = KK + 4
    VV = QQ + 4
    MG = VV + 4
    WO = MG + 24
    GU2 = WO + 4
    DN2 = GU2 + FC
    END = DN2 + 12
    MULT_AT = ZZ[0]
    TOK_AT = XBC[1]
    SCAN_AT = ZZ[0:2]
    YC_AT = [ZZ[2], ZZ[3]]
    CB_AT = XBC[2] + 2
    XTR_AT = [CB_AT + 1 + p for p in range(4)]
    SS = KK
    LOADS = [1] * END
    for n in [FDT, *range(GU1, DN1), *range(MG, WO), *range(GU2, DN2)]:
        LOADS[n] = 2
    ORDER = [2, 1, 0]
    OUT_PARTS = ((0, 2), (2, 4), (4, 6), (6, 8))
    YT_AT = {MG + 8: 0, MG + 9: 1, MG + 12: 2, MG + 15: 3}

    def arrived(n):
        return 16 * sum(LOADS[n % RING:n + 1:RING])

    def width(n):
        for d in (DN1, DN2):
            if d <= n < d + 12 and (n - d) % 3 == 2:
                return (FC - 16) * 2 * P
        return SLAB

    with ExitStack() as ctx:
        def sb(name, shape, dt=F32, st=ctx):
            return st.enter_context(nc.sbuf_tensor(name, shape, dt))

        def sem(name):
            return ctx.enter_context(nc.semaphore(name))

        raw = sb("raw", [P, RING, SLAB])
        whi = sb("whi", [P, RING, SLAB], F32R)
        wlo = sb("wlo", [P, RING, SLAB], F32R)
        xres = sb("xres", [P, C, T])
        thi = sb("act_hi", [P, C, T], F32R)
        tlo = sb("act_lo", [P, C, T], F32R)
        hn = sb("hn", [P, RING, T])
        acc = sb("acc", [P, T])
        rstd = sb("rstd", [P, T])
        ident = sb("ident", [P, P])
        ones = sb("ones", [P, P])
        sel = sb("sel", [48, 48], F32R)
        identb = sb("identb", [P, P], BF16)
        mask_qk = sb("mask_qk", [P, P], BF16)
        mask_st = sb("mask_st", [P, P], BF16)
        mask_s0 = sb("mask_s0", [P, P], BF16)
        colA = sb("colA", [P, 100])
        colB = sb("colB", [P, 64])
        small = sb("small", [P, 48])
        eps = sb("eps", [P, 1])
        dcol = sb("dcol", [P, C])
        scl48 = sb("scl48", [48, 4])

        with ExitStack() as s1:
            sq = sb("sq", [P, C, T], F32, s1)
            tokio = sb("tokio", [P, 2, D], F32, s1)
            metain = sb("metain", [META, D], F32, s1)
            rows = sb("rows", [P, 2, P], F32, s1)
            stmp = sb("stmp", [P, RING, T], F32, s1)
            hid_hi = sb("hid_hi", [P, FC, T], F32R, s1)
            hid_lo = sb("hid_lo", [P, FC, T], F32R, s1)

        XC = sb("xc_kt", [P, C, T])
        G = sb("gelu_qt", [P, C, TQ])
        XBCV = sb("xbc_v", [P, 12, T])
        Z = sb("z_mix", [P, C, TQ])
        XDV = sb("xdt_ytok", [P, 3 * D])
        y0hi = sb("y0hi", [P, C, TQ], F32R)
        y0lo = sb("y0lo", [P, C, TQ], F32R)
        craw = sb("craw", [P, 2, 2, T + 3])
        th = sb("th", [P, 2, T])
        work = sb("work", [P, 2560])
        cs_hi = sb("cs_hi", [48, T], F32R)
        cs_lo = sb("cs_lo", [48, T], F32R)
        tokm = sb("tokm", [P, 192])
        toka = sb("toka", [META, 96])
        with ExitStack() as s2:
            y1hi = sb("y1hi", [P, C, TQ], F32R, s2)
            y1lo = sb("y1lo", [P, C, TQ], F32R, s2)
        with ExitStack() as s3:
            bda = sb("bda", [P, C, P], F32, s3)
            bdx = sb("bdx", [P, C, P], F32, s3)
            la = sb("la", [P, 4, T], F32, s3)

        KT, QT = XC, G
        XT = XBCV
        V = XBCV[:, :, :].rearrange("p c t -> p (c t)")
        VM = V[:, 0:2 * D].rearrange("p (j d) -> p j d", j=2)
        VA = V[0:META, 2 * D:3 * D]
        XDM = XDV[:, 0:2 * D].rearrange("p (j d) -> p j d", j=2)
        XDA = XDV[0:META, 2 * D:3 * D]
        YA = XDV[:, 0:2 * D].rearrange("p (c t) -> p c t", c=C)
        MIX = Z
        zf = Z[:, :, :].rearrange("p c t -> p (c t)")
        xt48, e48, u48, l48, one48, sp48, cs48 = (XDV[0:48, k * T:(k + 1) * T] for k in range(7))
        ablk = u48[32:48, 0:TQ]
        thr = work[:, 0:2 * T].rearrange("p (j t) -> p j t", j=2)
        thx = work[:, 2 * T:4 * T].rearrange("p (j t) -> p j t", j=2)
        lv = work[:, 4 * T:8 * T].rearrange("p (j t) -> p j t", j=4)
        lv2 = XDV[:, 7 * T:11 * T].rearrange("p (j t) -> p j t", j=4)
        lvs = (lv, lv2)
        las = [la[:, c, :] for c in range(4)] + [zf[:, 4 * TQ + T * c:4 * TQ + T * (c + 1)] for c in range(3)]\
            + [rstd[:, :]]
        CB = work[:, 0:2 * W01].rearrange("p (g t) -> p g t", g=2)
        CBA = work[0:META, 2 * W01:2 * W01 + 2 * META].rearrange("p (g t) -> p g t", g=2)
        E = work[:, 2 * W01 + 2 * META:4 * W01 + 2 * META].rearrange("p (b t) -> p b t", b=2)
        EA = work[0:META, 4 * W01 + 2 * META:4 * W01 + (2 + H) * META].rearrange("p (h t) -> p h t", h=H)
        PR = work[:, 0:832].rearrange("p (b t) -> p b t", b=2)
        PT = work[:, 832:1600].rearrange("p (b t) -> p b t", b=2)
        PTA = work[0:META, 1600:2112].rearrange("p (b t) -> p b t", b=2)
        RS = work[:, 2112:2144]
        NM = work[:, 2144:2176]
        RI = work[:, 2176:2208]
        crf = craw[:, :, :, :].rearrange("p a b t -> p (a b t)")
        ytmp, ysq = crf[:, 0:TQ], crf[:, TQ:2 * TQ]
        mt = hn

        cA = {}
        at = 0
        for name, k in (("ffn1_norm", 8), ("mix_norm", 8), ("ffn2_norm", 8), ("final_norm", 8), ("ssd_norm", 8),
                        ("ssd_conv_b", 12), ("ssd_conv_w", 48)):
            cA[name] = at
            at += k
        nA = at
        cB = {}
        at = 0
        for name, k in (("lru_conv_w", 32), ("lru_conv_b", 8), ("lru_b_a", 8), ("lru_b_x", 8), ("lru_lambda", 8)):
            cB[name] = at
            at += k
        nB = at

        def col(name, k):
            return (colA[:, cA[name] + k:cA[name] + k + 1] if name in cA else
                    colB[:, cB[name] + k:cB[name] + k + 1])

        ba2, bx2, cpos, cneg, lam_e, lam_l = (small[:, 8 * k:8 * k + 8] for k in range(6))
        lam = colB[:, cB["lru_lambda"]:cB["lru_lambda"] + 8]

        banks = ctx.enter_context(nc.psum_tensor("banks", [P, 8, 512], F32))

        raw_in = [sem(f"raw_in{s}") for s in range(RING)]
        hi_done = sem("hi_done")
        lo_done = sem("lo_done")
        tiles_done = sem("tiles_done")
        evac = [sem("evac0"), sem("evac1")]
        x_in = sem("x_in")
        vec_in = sem("vec_in")
        lru_w_in = sem("lru_w_in")
        sml_in = sem("sml_in")
        consts = sem("consts")
        eps_set = sem("eps_set")
        scl_zero = sem("scl_zero")
        scl_ready = sem("scl_ready")
        lru_p = sem("lru_p")
        bd_zero = sem("bd_zero")
        pool_own = sem("pool_own")
        act_own = sem("act_own")
        dve_own = sem("dve_own")
        xt_done = sem("xt_done")
        vt_done = sem("vt_done")
        cols_done = sem("cols_done")
        x_new = sem("x_new")
        sq_done = sem("sq_done")
        sq_sum = sem("sq_sum")
        stat_done = sem("stat_done")
        rstd_done = sem("rstd_done")
        hn_done = sem("hn_done")
        nhi_done = sem("nhi_done")
        act_ready = sem("act_ready")
        silu_done = sem("silu_done")
        h_done = sem("h_done")
        hhi_done = sem("hhi_done")
        hlo_done = sem("hlo_done")
        lam_act = sem("lam_act")
        lam_dve = sem("lam_dve")
        fdt_act = sem("fdt_act")
        fdt_dve = sem("fdt_dve")
        fdt_tr = sem("fdt_tr")
        tok_ready = sem("tok_ready")
        cs_rounded = sem("cs_rounded")
        cs_split = sem("cs_split")
        sel_done = sem("sel_done")
        conv_done = sem("conv_done")
        lru_mm = sem("lru_mm")
        lru_acted = sem("lru_acted")
        gate_arg = sem("gate_arg")
        gate_th = sem("gate_th")
        gate_done = sem("gate_done")
        lru_a = sem("lru_a")
        lru_v = sem("lru_v")
        lru_mult = sem("lru_mult")
        lru_scan = sem("lru_scan")
        lru_h = sem("lru_h")
        yc_hi = sem("yc_hi")
        yc_ready = sem("yc_ready")
        xbc_th = sem("xbc_th")
        xbc_ready = sem("xbc_ready")
        z_th = sem("z_th")
        x_tr = sem("x_tr")
        xdt_done = sem("xdt_done")
        cb_mm = sem("cb_mm")
        cb_done = sem("cb_done")
        dec_mm = sem("dec_mm")
        dec_exp = sem("dec_exp")
        w_done = sem("w_done")
        ea_sum = sem("ea_sum")
        ea_exp = sem("ea_exp")
        ea_done = sem("ea_done")
        y_done = sem("y_done")
        y_evac = sem("y_evac")
        ysq_done = sem("ysq_done")
        gstat = sem("gstat")
        grs_done = sem("grs_done")
        yb_scaled = sem("yb_scaled")
        yb_hi = sem("yb_hi")
        yb_ready = sem("yb_ready")
        v_tr = sem("v_tr")
        v_main = sem("v_main")
        v_meta = sem("v_meta")
        s_mm = sem("s_mm")
        s_max = sem("s_max")
        s_exp = sem("s_exp")
        p_norm = sem("p_norm")
        p_tr = sem("p_tr")
        pt_main = sem("pt_main")
        pt_meta = sem("pt_meta")
        av_mm = sem("av_mm")
        ya_copied = sem("ya_copied")
        ya_hi = sem("ya_hi")
        ya_ready = sem("ya_ready")
        mg_th = sem("mg_th")
        mix_new = sem("mix_new")
        mix_hi = sem("mix_hi")
        mix_ready = sem("mix_ready")
        o_tr = sem("o_tr")
        o_act = sem("o_act")
        o_dve = sem("o_dve")
        stored = sem("stored")

        def rounds(eng, first, count, step):
            turns = count // RING
            if turns > 1:
                with eng.Fori(0, turns) as i:
                    for j in range(RING):
                        step(i * RING + (first + j), (first + j) % RING,
                         i * (16 * LOADS[first]) + arrived(first + j), i, j)
            else:
                turns = 0
            for n in range(first + RING * turns, first + count):
                step(n, n % RING, arrived(n), (n - first) // RING, (n - first) % RING)

        def pj(n):
            return 2 * (n % 2)

        def freed(n):
            return (n - FIRST) // 2 + 1

        def vectors(eng, tile, cols, names):
            for name in names:
                v = a[name]
                if name == "final_norm":
                    src = v.rearrange("(c p) -> c p", p=P)
                elif v.ndim == 3:
                    src = v[0].rearrange("k (c p) -> (k c) p", p=P)
                else:
                    src = v[0].rearrange("(c p) -> c p", p=P)
                eng.dma_start(rows[cols[name]:cols[name] + src.shape[0], tile, :], src).then_inc(vec_in, 16)

        def attn_lo(dve, g):
            dve.wait_ge(ya_hi, g + 1)
            dve.tensor_tensor(y0lo[:, 2 * g:2 * g + 2, :], YA[:, 2 * g:2 * g + 2, :],
                              y0hi[:, 2 * g:2 * g + 2, :].bitcast(F32), ALU.subtract).then_inc(ya_ready, 1)

        def attn_hi(act, g):
            act.wait_ge(ya_copied, g + 1)
            act.activation(y0hi[:, 2 * g:2 * g + 2, :], YA[:, 2 * g:2 * g + 2, :], ACT.Copy).then_inc(ya_hi, 1)

        def attn_values(pe, h):
            b, o = h % 2, TQ * (h // 2 % 2)
            hs = slice(DH * h, DH * (h + 1))
            pe.wait_ge(pt_main, h + 1)
            pe.wait_ge(pt_meta, h + 1)
            if h == 0:
                pe.wait_ge(v_main, 4)
                pe.wait_ge(v_meta, 4)
            elif h % 4 == 0:
                pe.wait_ge(ya_copied, h // 4)
            y = banks[DH * b:DH * (b + 1), 4, o:o + TQ]
            pe.matmul(y, VA[:, hs], PTA[:, b, :], start=True, stop=False)
            pe.matmul(y, VM[:, 0, hs], PT[:, b, 0:TQ], start=False, stop=False)
            pe.matmul(y[:, P:TQ], VM[:, 1, hs], PT[:, b, TQ:TQ + P], start=False, stop=True).then_inc(av_mm, 1)

        def to_tokens(pe, src, tiles, rest):
            for c in range(2):
                for j, ts in enumerate(tiles):
                    pe.transpose(banks[:, 4, 2 * P * c + P * j:2 * P * c + P * (j + 1)], src(c, ts), ident[:, :])
                last = pe.transpose(banks[0:META, 5, P * c:P * (c + 1)], src(c, rest), ident[:, :])
            return last

        block = ctx.enter_context(nc.Block())

        @block.sync
        def _(sp):
            def dst(slot, kcs=KC):
                return raw[:, slot, 0:kcs * 2 * P].rearrange("p (c n) -> p c n", c=kcs)

            def reuse(n):
                sp.wait_ge(lo_done, n + 1 - RING)

            def head_numbers():
                sp.wait_ge(scl_zero, 1)
                sp.dma_start(scl48[0:H, 0:1], a["fox_forget_bias"].rearrange("a h -> h a"),
                              allow_slow_non_contiguous=True).then_inc(sml_in, 16)
                sp.dma_start(scl48[32:48, 0:1], a["ssd_dt_bias"].rearrange("a h -> h a"),
                              allow_slow_non_contiguous=True).then_inc(sml_in, 16)
                sp.dma_start(scl48[32:48, 2:3], a["ssd_a_log"].rearrange("a h -> h a"),
                              allow_slow_non_contiguous=True).then_inc(sml_in, 16)
                for two in range(2):
                    sp.dma_start(dcol[DH * two:DH * (two + 1), :],
                                  a["ssd_d"].rearrange("a (c two) -> a two c", two=2)[:, two].broadcast_to([DH, C]),
                                  allow_slow_non_contiguous=True)\
                       .then_inc(sml_in, 16)

            def ffn(w_gu, w_dn, first, peel):
                gu = w_gu.rearrange("(c p) (two f) -> p c two f", p=P, two=2)
                dn = w_dn.rearrange("(c p) n -> p c n", p=P)

                def gate_up(n, slot, _arr, turn, j, base=first):
                    m = n - base
                    if not (isinstance(n, int) and n < RING):
                        reuse(n)
                    for two in range(2):
                        sp.dma_start(dst(slot)[:, :, two * P:(two + 1) * P], gu[:, :, two, bass.ds(m * P, P)])\
                          .then_inc(raw_in[slot], 16)

                for n in range(first, first + peel):
                    gate_up(n, n % RING, 0, 0, 0)
                    if n == 0:
                        vectors(sp, 1, cB, ("lru_conv_w", "lru_conv_b", "lru_b_a", "lru_b_x", "lru_lambda"))
                    if n == peel - 1:
                        head_numbers()
                rounds(sp, first + peel, FC - peel, gate_up)

                def down(n, slot, _arr, turn, j):
                    kcs = FC - 16 if j == 2 else KC
                    reuse(n)
                    sp.dma_start(dst(slot, kcs), dn[:, 8 * j:8 * j + kcs, bass.ds(turn * 2 * P, 2 * P)])\
                      .then_inc(raw_in[slot], 16)

                rounds(sp, first + FC, 12, down)

            ffn(a["ffn1_w_gate_up"][0], a["ffn1_w_down"][0], GU1, RING)

            win = w_in.rearrange("(c p) n -> p c n", p=P)

            def load(n, src):
                reuse(n)
                sp.dma_start(dst(n % RING), src).then_inc(raw_in[n % RING], 16)

            sources = {}
            for slabs, o in ((XR, oxr), (GATE, ogate), (sorted(XBC, key=XBC_PAIR.get), oxbc), (ZZ, oz),
                             (range(KK, QQ), ok), (range(QQ, VV), oq), (range(VV, MG), ov)):
                for j, n in enumerate(slabs):
                    sources[n] = o + 2 * P * j
            for n in range(FIRST, MG):
                if n == FDT:
                    reuse(n)
                    for at, o in ((0, of), (32, odt)):
                        sp.dma_start(dst(n % RING)[:, :, at:at + H], win[:, :, o:o + H]).then_inc(raw_in[n % RING], 16)
                else:
                    load(n, win[:, :, sources[n]:sources[n] + 2 * P])
            branch = [a["w_branch_attn"][0], a["w_branch_ssd"][0], a["w_branch_lru"][0]]
            for k in range(24):
                b, m, n = ORDER[k // C], k % C, MG + k
                reuse(n)
                sp.dma_start(dst(n % RING)[:, :, 0:P], win[:, :, omerge + b * D + m * P:omerge + b * D + (m + 1) * P])\
                  .then_inc(raw_in[n % RING], 16)
                sp.dma_start(dst(n % RING)[:, :, P:2 * P],
                             branch[b].rearrange("(c p) n -> p c n", p=P)[:, :, m * P:(m + 1) * P])\
                  .then_inc(raw_in[n % RING], 16)
            for j in range(4):
                load(WO + j, a["w_out"][0].rearrange("(c p) n -> p c n", p=P)[:, :, 2 * P * j:2 * P * (j + 1)])
            ffn(a["ffn2_w_gate_up"][0], a["ffn2_w_down"][0], GU2, 0)

            for i, (c, e) in enumerate(OUT_PARTS):
                sp.wait_ge(o_act, i + 1)
                if e == C:
                    sp.wait_ge(o_dve, 1)
                sp.dma_start(out[0].rearrange("(j p) d -> p j d", p=P)[:, :, P * c:P * e],
                             tokio[:, :, P * c:P * e]).then_inc(stored, 16)
            sp.wait_ge(stored, 16 * len(OUT_PARTS))

        @block.gpsimd
        def _(pool):
            own = Own(pool, pool_own)
            own.did(pool.memset(ident[:, :], 0.0))
            own.did(pool.memset(mask_qk[:, :], 0.0))
            own.did(pool.memset(mask_st[:, :], 0.0))
            own.did(pool.memset(mask_s0[:, :], 0.0))
            pool.memset(ones[:, :], 1.0).then_inc(consts, 1)
            own.settle()
            own.did(pool.affine_select(out=ident[:, :], in_=ident[:, :], pattern=[[-1, P]],
                                       compare_op=ALU.not_equal, fill=1.0, base=0, channel_multiplier=1))
            pool.affine_select(out=mask_qk[:, :], in_=mask_qk[:, :], pattern=[[-1, P]],
                               compare_op=ALU.is_ge, fill=NEG, base=0, channel_multiplier=1).then_inc(consts, 1)
            pool.affine_select(out=mask_st[:, :], in_=mask_st[:, :], pattern=[[1, P]],
                               compare_op=ALU.is_ge, fill=NEG, base=0, channel_multiplier=-1).then_inc(consts, 1)
            pool.affine_select(out=mask_s0[:, :], in_=mask_s0[:, :], pattern=[[1, P]],
                               compare_op=ALU.is_ge, fill=NEG, base=META, channel_multiplier=-1).then_inc(consts, 1)
            own.settle()
            pool.tensor_copy(identb[:, :], ident[:, :]).then_inc(consts, 1)
            pool.tensor_copy(sel[:, :], ident[0:48, 0:48]).then_inc(sel_done, 1)
            pool.memset(bda[:, :, :], 0.0).then_inc(bd_zero, 1)
            pool.memset(bdx[:, :, :], 0.0).then_inc(bd_zero, 1)
            pool.wait_ge(bd_zero, 2)
            for bd, w in ((bda, a["lru_w_a"][0]), (bdx, a["lru_w_x"][0])):
                for two in range(2):
                    pool.dma_start(bd[DH * two:DH * (two + 1), :, DH * two:DH * (two + 1)],
                                   w.rearrange("(t two) i j -> i two t j", two=2)[:, two]).then_inc(lru_w_in, 16)

            def sum_squares(q, cols):
                for k in range(3):
                    pool.wait_ge(sq_done, 4 * q + k + 1)
                    for c in (2 * k, 2 * k + 1):
                        if c == 0:
                            continue
                        if c == 1:
                            pool.wait_ge(stat_done, q)
                        if c == 1 and q == 2:
                            pool.wait_ge(yb_scaled, 2)
                        first = sq[:, 0, cols] if c == 1 else acc[:, cols]
                        ins = pool.tensor_tensor(acc[:, cols], first, sq[:, c, cols], ALU.add)
                        if c == 5:
                            ins.then_inc(sq_sum, 1)
                        else:
                            own.did(ins)
                            own.settle()

            sum_squares(1, ALL)
            sum_squares(2, OUTS)
            sum_squares(3, OUTS)

        @block.scalar
        def _(act):
            own = Own(act, act_own)

            act.dma_start(tokio[:, :, :], a["x"][0].rearrange("(j p) d -> p j d", p=P)).then_inc(x_in, 16)
            act.dma_start(metain[:, :], a["meta_tokens"]).then_inc(x_in, 16)
            vectors(act, 0, cA, ("ffn1_norm", "mix_norm", "ffn2_norm", "final_norm", "ssd_norm", "ssd_conv_b",
                                 "ssd_conv_w"))

            def split(n, slot, arr, w):
                act.wait_ge(raw_in[slot], arr)
                if not (isinstance(n, int) and n < RING):
                    act.wait_ge(tiles_done, 2 * (n - RING) + 2)
                act.activation(whi[:, slot, 0:w], raw[:, slot, 0:w], ACT.Copy).then_inc(hi_done, 1)

            def split_at(n):
                if n < END:
                    split(n, n % RING, arrived(n), width(n))

            def squares(q, k, cols):
                act.wait_ge(x_new, C * q + 2 * k + 2)
                act.activation(sq[:, 2 * k:2 * k + 2, cols], xres[:, 2 * k:2 * k + 2, cols], ACT.Square)\
                   .then_inc(sq_done, 1)

            def norm(q, cols):
                act.preload_act_table_set(LN_EXP)
                act.wait_ge(stat_done, q + 1)
                own.did(act.activation(rstd[:, cols], banks[:, 7, 0:cols.stop - cols.start], ACT.Ln,
                                       bias=eps[:, 0:1], scale=1.0 / D))
                own.settle()
                act.activation(rstd[:, cols], rstd[:, cols], ACT.Exp, scale=-0.5).then_inc(rstd_done, 1)
                if q < 3:
                    for c in range(C):
                        act.wait_ge(hn_done, C * q + c + 1)
                        act.activation(thi[:, c, cols], hn[:, c % RING, 0:cols.stop - cols.start], ACT.Copy)\
                           .then_inc(nhi_done, 1)
                        if q == 0 and c % 2 == 0:
                            if c == 0:
                                act.wait_ge(raw_in[1], arrived(1))
                            quarter = slice(SLAB // C * c, SLAB // C * (c + 2))
                            ins = act.activation(whi[:, 1, quarter], raw[:, 1, quarter], ACT.Copy)
                            if c == C - 2:
                                ins.then_inc(hi_done, 1)

            for k in range(4):
                squares(0, k, ALL)
            split_at(0)
            act.wait_ge(eps_set, 1)
            norm(0, ALL)
            split_at(2)
            own.did(act.activation(lam_e, lam, ACT.Abs))
            own.settle()
            act.activation(lam_e, lam_e, ACT.Exp, scale=-1.0).then_inc(lam_act, 1)
            act.wait_ge(sml_in, 80)
            act.activation(scl48[32:48, 3:4], scl48[32:48, 2:3], ACT.Exp).then_inc(lam_act, 1)
            act.wait_ge(lam_dve, 1)
            act.activation(lam_l, cpos, ACT.Ln).then_inc(lam_act, 1)

            def ffn(q, first, cols, base):
                w = cols.stop - cols.start

                def gate_up(n, slot, arr, turn, j, wide=None, m=None):
                    m = n - first if m is None else m
                    act.wait_ge(tiles_done, 2 * n + 1)
                    if not (isinstance(n, int) and n < RING):
                        act.wait_ge(h_done, m + (base - RING + 1))
                    act.activation(stmp[:, slot, 0:w], banks[:, 2 * slot, 0:w], ACT.Silu).then_inc(silu_done, 1)
                    nxt = arrived(n + RING) if isinstance(n, int) else arr + 16 * LOADS[first]
                    split(n + RING, slot, nxt, SLAB if wide is None else wide)
                    act.wait_ge(h_done, m + (base + 1))
                    act.activation(hid_hi[:, m, cols] if isinstance(m, int) else hid_hi[:, bass.ds(m, 1), cols],
                                   (hn[:, slot, 0:w] if isinstance(m, int) else hn[:, slot:slot + 1, 0:w]),
                                   ACT.Copy).then_inc(hhi_done, 1)

                peel = RING if first == 0 else 0
                for n in range(first, first + peel):
                    gate_up(n, n % RING, arrived(n), 0, 0)
                rounds(act, first + peel, FC - RING - peel, gate_up)
                for n in range(first + FC - RING, first + FC):
                    gate_up(n, n % RING, arrived(n), 0, 0, wide=width(n + RING))

                d0 = first + FC

                def down(n, slot, arr, turn, j, ahead=True):
                    if j == 2:
                        squares_dyn(turn)
                    if ahead:
                        split(n + RING, slot, arr + 16, (FC - 16) * 2 * P if j == 2 else SLAB)

                def squares_dyn(turn):
                    act.wait_ge(x_new, turn * 2 + (C * q + 2))
                    if isinstance(turn, int):
                        o, i = sq[:, 2 * turn:2 * turn + 2, cols], xres[:, 2 * turn:2 * turn + 2, cols]
                    else:
                        o, i = sq[:, bass.ds(turn * 2, 2), cols], xres[:, bass.ds(turn * 2, 2), cols]
                    act.activation(o, i, ACT.Square).then_inc(sq_done, 1)

                rounds(act, d0, 9, down)
                for j in range(RING):
                    down(d0 + 9 + j, (d0 + 9 + j) % RING, 0, 3, j, ahead=False)
                    if j < 2:
                        split_at(d0 + 12 + j)

            ffn(1, GU1, ALL, 0)
            norm(1, ALL)
            split_at(FIRST + 2)

            def conv_evac(n, i, name_w, name_b, c0, dest, stride):
                if i >= 2:
                    act.wait_ge(conv_done, i - 1)
                for t in range(2):
                    act.activation(dest[:, c0 + t, :], banks[:, pj(n) + t, 0:T], ACT.Identity,
                                   scale=col(name_w, 3 * stride + c0 + t), bias=col(name_b, c0 + t))
                    ins = act.activation(craw[:, i % 2, t, 3:3 + T], banks[:, pj(n) + t, 0:T], ACT.Copy)
                ins.then_inc(evac[n % 2], 1)

            def decay_exps(i):
                for b in range(2):
                    h = 2 * i + b
                    act.wait_ge(dec_mm, h + 1)
                    if i > 0:
                        act.wait_ge(y_done, i)
                    act.activation(E[:, b, 0:TQ], banks[:, 4 + b, 0:TQ], ACT.Exp, bias=tokm[:, 128 + h:129 + h])
                    act.activation(E[:, b, TQ:W01], banks[:, 4 + b, TQ:W01], ACT.Exp,
                                   bias=tokm[:, 176 + h:177 + h]).then_inc(dec_exp, 1)

            for n in range(FIRST, GU2):
                act.wait_ge(tiles_done, 2 * n + 2)
                if n == FDT:
                    act.wait_ge(scl_ready, 1)
                    act.activation(xt48, banks[0:48, pj(n), 0:T], ACT.Identity, scale=scl48[:, 1:2],
                                   bias=scl48[:, 0:1]).then_inc(evac[n % 2], 1)
                elif n in XR:
                    conv_evac(n, XR.index(n), "lru_conv_w", "lru_conv_b", 2 * XR.index(n), XC, C)
                elif n in GATE:
                    j = GATE.index(n)
                    if j > 0:
                        act.wait_ge(gate_done, j)
                    src = banks[:, pj(n):pj(n) + 2, 0:TQ]
                    act.activation(th[:, :, 0:TQ], src, ACT.Square, scale=float(np.sqrt(GELU_C)))
                    act.activation(G[:, 2 * j:2 * j + 2, :], src, ACT.Copy).then_inc(evac[n % 2], 1)
                elif n in XBC:
                    conv_evac(n, 4 + XBC.index(n), "ssd_conv_w", "ssd_conv_b", 2 * XBC_PAIR[n], XT, 12)
                elif n in ZZ:
                    j = ZZ.index(n)
                    act.activation(Z[:, 2 * j:2 * j + 2, :], banks[:, pj(n):pj(n) + 2, 0:TQ], ACT.Tanh, scale=0.5)\
                       .then_inc(z_th, 1)
                elif QQ <= n < VV:
                    j = n - QQ
                    act.wait_ge(yc_ready, 2)
                    act.activation(QT[:, 2 * j:2 * j + 2, :], banks[:, pj(n):pj(n) + 2, 0:TQ], ACT.Copy,
                                   scale=float(DH) ** -0.5).then_inc(evac[n % 2], 1)
                elif KK <= n < QQ:
                    j = n - KK
                    act.wait_ge(lru_h, 2)
                    act.activation(KT[:, 2 * j:2 * j + 2, :], banks[:, pj(n):pj(n) + 2, 0:T], ACT.Copy)\
                       .then_inc(evac[n % 2], 1)
                elif VV <= n < MG:
                    j = n - VV
                    if j > 0:
                        act.wait_ge(v_tr, j)
                    else:
                        act.wait_ge(xbc_ready, 6)
                    act.activation(th[:, :, :], banks[:, pj(n):pj(n) + 2, 0:T], ACT.Copy).then_inc(evac[n % 2], 1)
                elif MG <= n < WO:
                    k = n - MG
                    if k >= 2:
                        act.wait_ge(evac[n % 2], freed(n - 2))
                    act.activation(mt[:, k % 2, 0:TQ], banks[:, pj(n), 0:TQ], ACT.Tanh, scale=0.5)\
                       .then_inc(mg_th, 1)

                if n in LRU_AT:
                    split_at(n + RING)
                if n == FDT:
                    act.preload_act_table_set(LN_EXP)
                    act.wait_ge(evac[FDT % 2], freed(FDT))
                    own.did(act.activation(e48, xt48, ACT.Abs))
                    own.settle()
                    act.activation(e48, e48, ACT.Exp, scale=-1.0).then_inc(fdt_act, 1)
                    act.wait_ge(fdt_dve, 1)
                    act.activation(l48, u48, ACT.Ln).then_inc(fdt_act, 1)
                if n == TOK_AT:
                    act.wait_ge(fdt_dve, 2)
                    act.activation(cs_hi[:, :], cs48, ACT.Copy).then_inc(cs_rounded, 1)
                    act.wait_ge(fdt_tr, 1)
                    act.activation(tokm[:, 0:96], banks[:, 7, 0:96], ACT.Copy, scale=0.25)
                    act.activation(tokm[:, 96:192], banks[:, 7, 96:192], ACT.Copy, scale=-1.0)
                    act.activation(toka[:, 0:48], banks[0:META, 7, 192:240], ACT.Copy, scale=0.25)
                    act.activation(toka[:, 48:96], banks[0:META, 7, 240:288], ACT.Copy, scale=-1.0)\
                       .then_inc(tok_ready, 1)
                if n == MULT_AT:
                    act.preload_act_table_set(LN_EXP)
                    for half in range(2):
                        act.wait_ge(lru_v, half + 1)
                        own.did(act.activation(lvs[half], lvs[half], ACT.Ln, scale=1.0 / 16))
                    for half in range(2):
                        own.settle(own.n - 1 + half)
                        act.activation(lvs[half], lvs[half], ACT.Exp, scale=0.5).then_inc(lru_mult, 1)
                if n - 3 in YC_AT:
                    half = YC_AT.index(n - 3)
                    act.wait_ge(lru_h, half + 1)
                    act.activation(y0hi[:, 4 * half:4 * half + 4, :], G[:, 4 * half:4 * half + 4, :], ACT.Copy)\
                       .then_inc(yc_hi, 1)
                if n in LRU_AT:
                    i = LRU_AT.index(n)
                    act.wait_ge(lru_mm, i + 1)
                    if i > 0:
                        act.wait_ge(lru_p, i)
                    for t in range(2):
                        c = 2 * i + t
                        act.activation(thr[:, t, :], banks[:, 4 + 2 * t, 0:T], ACT.Tanh, scale=0.5,
                                       bias=ba2[:, c:c + 1])
                        ins = act.activation(thx[:, t, :], banks[:, 5 + 2 * t, 0:T], ACT.Tanh, scale=0.5,
                                             bias=bx2[:, c:c + 1])
                    ins.then_inc(lru_acted, 1)
                    act.wait_ge(lru_acted, i + 1)
                    for t in range(2):
                        c = 2 * i + t
                        act.activation(las[c], thr[:, t, :], ACT.Exp, scale=cpos[:, c:c + 1],
                                       bias=cpos[:, c:c + 1])
                        ins = act.activation(lvs[c // 4][:, c % 4, :], thr[:, t, :], ACT.Tanh, scale=cneg[:, c:c + 1],
                                             bias=cneg[:, c:c + 1])
                    ins.then_inc(lru_a, 1)
                if n in GATE:
                    act.wait_ge(gate_arg, GATE.index(n) + 1)
                    act.activation(th[:, :, 0:TQ], th[:, :, 0:TQ], ACT.Tanh, scale=GELU_S).then_inc(gate_th, 1)
                if n - 1 in XBC:
                    i = XBC.index(n - 1)
                    p = XBC_PAIR[n - 1]
                    act.wait_ge(conv_done, 5 + i)
                    if i > 0:
                        act.wait_ge(xbc_ready, i)
                    else:
                        act.wait_ge(gate_done, 4)
                    act.activation(th[:, :, :], XT[:, 2 * p:2 * p + 2, :], ACT.Tanh, scale=0.5).then_inc(xbc_th, 1)
                if n == CB_AT:
                    act.wait_ge(cb_mm, 1)
                    for g in range(2):
                        act.activation(CB[:, g, :], banks[:, 4 + 2 * g, 0:W01], ACT.Copy, scale=0.25)
                        ins = act.activation(CBA[:, g, :], banks[0:META, 5 + 2 * g, 0:META], ACT.Copy, scale=0.25)
                    ins.then_inc(cb_done, 1)
                if n == CB_AT + 1:
                    act.wait_ge(ea_sum, 1)
                    act.activation(EA, EA, ACT.Exp).then_inc(ea_exp, 1)
                if SS <= n < SS + 8:
                    if n == SS:
                        act.wait_ge(tok_ready, 1)
                        act.preload_act_table_set(LN_EXP)
                    decay_exps(n - SS)
                if n in (SS + 5, SS + 9):
                    g = (n - SS - 5) // 4
                    act.wait_ge(gstat, 4 * g + 4)
                    if g == 1:
                        act.wait_ge(yb_scaled, 1)
                    own.did(act.activation(acc[:, 0:TQ], banks[:, 7, 0:TQ], ACT.Ln, bias=eps[:, 0:1],
                                           scale=1.0 / (4 * P)))
                    own.settle()
                    act.activation(acc[:, 0:TQ], acc[:, 0:TQ], ACT.Exp, scale=-0.5).then_inc(grs_done, 1)
                if SS + 1 <= n < SS + 9:
                    c = n - SS - 1
                    if c > 0:
                        act.wait_ge(gstat, c)
                    act.wait_ge(y_evac, c + 1)
                    act.activation(ysq, Z[:, c, :], ACT.Square).then_inc(ysq_done, 1)
                if n in (SS + 6, SS + 10):
                    g = (n - SS - 6) // 4
                    act.wait_ge(yb_scaled, g + 1)
                    act.activation(y1hi[:, 4 * g:4 * g + 4, :], Z[:, 4 * g:4 * g + 4, :], ACT.Copy).then_inc(yb_hi, 1)
                if VV <= n < MG:
                    i = n - VV
                    act.wait_ge(v_tr, i + 1)
                    act.wait_ge(y_evac, C)
                    act.activation(VM[:, :, 2 * P * i:2 * P * (i + 1)].rearrange("p j (c x) -> p c j x", c=2),
                                   banks[:, 4, :].rearrange("p (c j x) -> p c j x", c=2, j=2),
                                   ACT.Copy).then_inc(v_main, 1)
                if VV + 2 <= n < VV + 19:
                    h = n - VV - 2
                    if h == 0:
                        act.preload_act_table_set(EXP_TANH)
                    if h < H:
                        act.wait_ge(s_max, h + 1)
                        if h >= 2:
                            act.wait_ge(p_tr, h - 1)
                        act.activation(PR[:, h % 2, 0:144], banks[:, 6, 0:144], ACT.Exp,
                                       bias=NM[:, 2 * h:2 * h + 1], accum_out=RS[:, 2 * h:2 * h + 1])
                        act.activation(PR[:, h % 2, 144:416], banks[:, 6, 144:416], ACT.Exp,
                                       bias=NM[:, 2 * h + 1:2 * h + 2], accum_out=RS[:, 2 * h + 1:2 * h + 2])\
                           .then_inc(s_exp, 1)
                    if h >= 1:
                        act.wait_ge(p_tr, h)
                        if h >= 3:
                            act.wait_ge(av_mm, h - 2)
                        act.activation(PT[:, (h - 1) % 2, :], banks[:, 7, 0:3 * P], ACT.Copy).then_inc(pt_main, 1)
                if n in YT_AT:
                    attn_hi(act, YT_AT[n])
                if MG + 16 <= n < WO:
                    m = n - MG - 16
                    act.wait_ge(mix_new, m + 1)
                    act.activation(y1hi[:, m, :], MIX[:, m, :], ACT.Copy, scale=0.5).then_inc(mix_hi, 1)
                if WO <= n < GU2:
                    squares(2, n - WO, OUTS)

                if n not in LRU_AT and n < GU2 - 1:
                    split_at(n + RING)

            norm(2, OUTS)
            split_at(GU2 + 2)
            ffn(3, GU2, OUTS, FC)
            norm(3, OUTS)
            for i, (c, e) in enumerate(OUT_PARTS):
                act.wait_ge(o_tr, e)
                j = 1 if e == C else 0
                act.activation(tokio[:, j:2, P * c:P * e], banks[:, 2 * i + j:2 * i + 2, 0:P * (e - c)], ACT.Copy)\
                   .then_inc(o_act, 1)

        @block.vector
        def _(dve):
            own = Own(dve, dve_own)

            def split(n, slot, w):
                dve.wait_ge(hi_done, n + 1)
                dve.tensor_tensor(wlo[:, slot, 0:w], raw[:, slot, 0:w], whi[:, slot, 0:w].bitcast(F32), ALU.subtract)\
                   .then_inc(lo_done, 1)

            def split_at(n):
                if n < END:
                    split(n, n % RING, width(n))

            def norm(q, gain, cols):
                w = cols.stop - cols.start
                dve.wait_ge(rstd_done, q + 1)
                for c in range(C + 1):
                    if c < C:
                        if q == 3 and c >= RING:
                            dve.wait_ge(o_tr, c + 1 - RING)
                        elif c >= RING:
                            dve.wait_ge(act_ready, C * q + c + 1 - RING)
                        dve.scalar_tensor_tensor(hn[:, c % RING, 0:w], xres[:, c, cols], col(gain, c), rstd[:, cols],
                                                 ALU.mult, ALU.mult).then_inc(hn_done, 1)
                    if c > 0 and q < 3:
                        dve.wait_ge(nhi_done, C * q + c)
                        dve.tensor_tensor(tlo[:, c - 1, cols], hn[:, (c - 1) % RING, 0:w],
                                          thi[:, c - 1, cols].bitcast(F32), ALU.subtract).then_inc(act_ready, 1)

            dve.memset(eps[:, :], EPS).then_inc(eps_set, 1)
            dve.memset(scl48[:, :], 0.0).then_inc(scl_zero, 1)
            for c in range(C):
                dve.wait_ge(xt_done, c + 1)
                dve.tensor_copy(xres[:, c, :], banks[:, c % 6, 0:T]).then_inc(x_new, 1)
            split_at(0)
            dve.wait_ge(vt_done, 1)
            dve.tensor_copy(colA[:, 0:nA], banks[:, 6, 0:nA]).then_inc(cols_done, 1)
            dve.tensor_copy(colB[:, 0:nB], banks[:, 6, P:P + nB]).then_inc(cols_done, 1)
            dve.wait_ge(cols_done, 2)
            norm(0, "ffn1_norm", ALL)
            for n in range(1, RING):
                split_at(n)

            dve.wait_ge(lam_act, 1)
            dve.tensor_scalar(cpos, lam_e, 1.0, None, ALU.add).then_inc(lam_dve, 1)
            own.did(dve.tensor_scalar(ba2, colB[:, cB["lru_b_a"]:cB["lru_b_a"] + 8], 0.5, None, ALU.mult))
            own.did(dve.tensor_scalar(bx2, colB[:, cB["lru_b_x"]:cB["lru_b_x"] + 8], 0.5, None, ALU.mult))
            dve.wait_ge(lam_act, 3)
            own.did(dve.tensor_scalar(cneg, cpos, 1.0, 1e-10, ALU.subtract, ALU.max))
            own.did(dve.tensor_scalar(lam_l, lam_l, 1e-10, None, ALU.max))
            own.settle()
            own.did(dve.reciprocal(cneg, cneg))
            own.did(dve.tensor_tensor(lam_l, lam_l, lam_e, ALU.mult))
            own.settle()
            own.did(dve.tensor_tensor(lam_l, lam_l, cneg, ALU.mult))
            own.did(dve.tensor_scalar(lam_e, lam, -1.0, 0.0, ALU.mult, ALU.max))
            own.settle()
            own.did(dve.tensor_tensor(lam_l, lam_l, lam_e, ALU.add))
            own.settle()
            own.did(dve.tensor_scalar(cpos, lam_l, -4.0, None, ALU.mult))
            own.did(dve.tensor_scalar(cneg, lam_l, 4.0, None, ALU.mult))
            dve.wait_ge(sml_in, 80)
            own.did(dve.tensor_scalar(dcol[:, :], dcol[:, :], 0.25, None, ALU.mult))
            own.did(dve.tensor_scalar(scl48[0:H, 0:1], scl48[0:H, 0:1], -1.0, None, ALU.mult))
            own.did(dve.memset(scl48[0:H, 1:2], -1.0))
            own.did(dve.memset(scl48[32:48, 1:2], 1.0))
            own.did(dve.memset(scl48[0:H, 3:4], 1.0))
            own.settle()
            dve.tensor_scalar(scl48[32:48, 3:4], scl48[32:48, 3:4], -1.0, None, ALU.mult).then_inc(scl_ready, 1)

            def ffn(q, first, cols, base):
                w = cols.stop - cols.start

                def one(t, m):
                    return t[:, m:m + 1, cols] if isinstance(m, int) else t[:, bass.ds(m, 1), cols]

                def gate_up(n, slot, arr, turn, j, wide=SLAB):
                    m = n - first
                    dve.wait_ge(silu_done, m + (base + 1))
                    dve.wait_ge(tiles_done, 2 * n + 2)
                    dve.tensor_tensor(hn[:, slot, 0:w], stmp[:, slot, 0:w], banks[:, 2 * slot + 1, 0:w], ALU.mult)\
                       .then_inc(h_done, 1)
                    split(n + RING, slot, wide)
                    dve.wait_ge(hhi_done, m + (base + 1))
                    dve.tensor_tensor(one(hid_lo, m), hn[:, slot:slot + 1, 0:w], one(hid_hi, m).bitcast(F32),
                                      ALU.subtract).then_inc(hlo_done, 1)

                rounds(dve, first, FC - RING, gate_up)
                for n in range(first + FC - RING, first + FC):
                    gate_up(n, n % RING, 0, 0, 0, wide=width(n + RING))

                def down(n, slot, arr, turn, j, ahead=True):
                    if j == 2:
                        for t in range(2):
                            dve.wait_ge(tiles_done, 2 * n + (1 + t))
                            x = one(xres, turn * 2 + t)
                            dve.scalar_tensor_tensor(x, banks[:, 2 + t:3 + t, 0:w], 0.5, x, ALU.mult, ALU.add)\
                               .then_inc(x_new, 1)
                        if ahead:
                            split(n + RING - 1, (slot - 1) % RING, SLAB)
                    if ahead and j != 1:
                        split(n + RING, slot, (FC - 16) * 2 * P if j == 2 else SLAB)

                d0 = first + FC
                rounds(dve, d0, 9, down)
                for j in range(RING):
                    down(d0 + 9 + j, (d0 + 9 + j) % RING, 0, 3, j, ahead=False)
                    if j == 0:
                        split_at(d0 + 12)

            ffn(1, GU1, ALL, 0)
            split_at(FIRST + 1)
            norm(1, "mix_norm", ALL)
            own.did(dve.memset(craw[:, :, :, 0:3], 0.0))
            split_at(FIRST + 2)
            own.settle()

            def conv(n, i, name_w, c0, dest, stride):
                dve.wait_ge(evac[n % 2], freed(n))
                for k in (2, 1, 0):
                    for t in range(2):
                        ins = dve.scalar_tensor_tensor(dest[:, c0 + t, :], craw[:, i % 2, t, k:k + T],
                                                       col(name_w, k * stride + c0 + t), dest[:, c0 + t, :],
                                                       ALU.mult, ALU.add)
                        if k > 0:
                            own.did(ins)
                    if k > 0:
                        own.settle()
                ins.then_inc(conv_done, 1)

            for n in range(FIRST, GU2):
                if n in ZZ:
                    j = ZZ.index(n)
                    dve.wait_ge(z_th, j + 1)
                    zp = Z[:, 2 * j:2 * j + 2, :]
                    dve.scalar_tensor_tensor(zp, zp, 1.0, banks[:, pj(n):pj(n) + 2, 0:TQ], ALU.add, ALU.mult)\
                       .then_inc(evac[n % 2], 1)
                elif MG <= n < WO:
                    k = n - MG
                    m = k % C
                    dve.wait_ge(mg_th, k + 1)
                    dve.wait_ge(tiles_done, 2 * n + 2)
                    dst = MIX[:, m, :] if k < C else hn[:, 2, 0:TQ]
                    if C < k <= 2 * C:
                        own.settle()
                    elif k > 2 * C:
                        dve.wait_ge(mix_new, k - 2 * C)
                    dve.scalar_tensor_tensor(dst, mt[:, k % 2, 0:TQ], 1.0, banks[:, pj(n) + 1, 0:TQ],
                                             ALU.add, ALU.mult).then_inc(evac[n % 2], 1)
                    if k >= C:
                        dve.wait_ge(evac[n % 2], freed(n))
                        ins = dve.tensor_tensor(MIX[:, m, :], MIX[:, m, :], dst, ALU.add)
                        if k >= 2 * C:
                            ins.then_inc(mix_new, 1)
                        else:
                            own.did(ins)
                elif n >= WO:
                    for t in range(2):
                        c = 2 * (n - WO) + t
                        dve.wait_ge(tiles_done, 2 * n + 1 + t)
                        dve.tensor_tensor(xres[:, c, OUTS], xres[:, c, OUTS], banks[:, pj(n) + t, 0:TQ], ALU.add)\
                           .then_inc(x_new, 1)

                if n == TOK_AT:
                    dve.tensor_tensor(ablk.rearrange("p (h t) -> p h t", h=H),
                                      cs48[32:48, S2].unsqueeze(1).broadcast_to([H, H, META]),
                                      ident[32:48, 32:48].unsqueeze(2).broadcast_to([H, H, META]), ALU.mult)
                    dve.wait_ge(cs_rounded, 1)
                    dve.tensor_tensor(cs_lo[:, :], cs48, cs_hi[:, :].bitcast(F32), ALU.subtract).then_inc(cs_split, 1)
                if n in XR:
                    conv(n, XR.index(n), "lru_conv_w", 2 * XR.index(n), XC, C)
                if n in GATE:
                    j = GATE.index(n)
                    dve.wait_ge(evac[n % 2], freed(n))
                    dve.scalar_tensor_tensor(th[:, :, 0:TQ], th[:, :, 0:TQ], 1.0, G[:, 2 * j:2 * j + 2, :],
                                             ALU.add, ALU.mult).then_inc(gate_arg, 1)
                if n - 1 in LRU_AT:
                    i = LRU_AT.index(n - 1)
                    v = lvs[i // 2]
                    dve.wait_ge(lru_a, i + 1)
                    for t in range(2):
                        c = 2 * i + t
                        own.did(dve.scalar_tensor_tensor(XC[:, c, :], thx[:, t, :], 1.0, XC[:, c, :],
                                                         ALU.add, ALU.mult))
                        own.did(dve.tensor_tensor(thr[:, t, :], las[c], las[c], ALU.mult))
                    own.settle()
                    for t in range(2):
                        c = 2 * i + t
                        ins = dve.scalar_tensor_tensor(v[:, c % 4, :], thr[:, t, :], 1.0, v[:, c % 4, :],
                                                       ALU.add, ALU.mult)
                    ins.then_inc(lru_p, 1)
                    if i % 2:
                        dve.wait_ge(lru_p, i + 1)
                        own.did(dve.tensor_scalar(v, v, 1e-16, None, ALU.max))
                        own.settle()
                        dve.memset(v[:, :, 0:1], 1.0).then_inc(lru_v, 1)
                if n in GATE:
                    j = GATE.index(n)
                    dve.wait_ge(gate_th, j + 1)
                    gp = G[:, 2 * j:2 * j + 2, :]
                    dve.scalar_tensor_tensor(gp, th[:, :, 0:TQ], 1.0, gp, ALU.add, ALU.mult).then_inc(gate_done, 1)
                if n == FDT:
                    dve.wait_ge(fdt_act, 1)
                    dve.tensor_scalar(u48, e48, 1.0, None, ALU.add).then_inc(fdt_dve, 1)
                    own.did(dve.memset(one48, 1.0))
                    dve.wait_ge(fdt_act, 2)
                    own.did(dve.tensor_scalar(u48, u48, 1.0, 1e-10, ALU.subtract, ALU.max))
                    own.did(dve.tensor_scalar(l48, l48, 1e-10, None, ALU.max))
                    own.settle()
                    own.did(dve.reciprocal(u48, u48))
                    own.did(dve.tensor_tensor(l48, l48, e48, ALU.mult))
                    own.settle()
                    own.did(dve.tensor_tensor(l48, l48, u48, ALU.mult))
                    own.settle()
                    own.did(dve.scalar_tensor_tensor(sp48, xt48, 0.0, l48, ALU.max, ALU.add))
                    own.settle()
                    own.did(dve.tensor_scalar(e48, sp48, scl48[:, 3:4], None, ALU.mult))
                    own.settle()
                    dve.tensor_tensor_scan(cs48, one48, e48, 0.0, ALU.mult, ALU.add).then_inc(fdt_dve, 1)
                if n in SCAN_AT:
                    half = SCAN_AT.index(n)
                    hs = slice(4 * half, 4 * half + 4)
                    dve.wait_ge(lru_mult, half + 1)
                    own.did(dve.tensor_tensor(lvs[half], lvs[half], XC[:, hs, :], ALU.mult))
                    own.settle()
                    for c in range(4):
                        ins = dve.tensor_tensor_scan(XC[:, 4 * half + c, :], las[4 * half + c], lvs[half][:, c, :], 0.0,
                                                     ALU.mult, ALU.add)
                    ins.then_inc(lru_scan, 1)
                if n in YC_AT:
                    half = YC_AT.index(n)
                    hs = slice(4 * half, 4 * half + 4)
                    dve.wait_ge(lru_scan, half + 1)
                    dve.wait_ge(gate_done, 2 * half + 2)
                    dve.tensor_tensor(G[:, hs, :], XC[:, hs, OUTS], G[:, hs, :], ALU.mult).then_inc(lru_h, 1)
                if n - 3 in YC_AT:
                    half = YC_AT.index(n - 3)
                    hs = slice(4 * half, 4 * half + 4)
                    dve.wait_ge(yc_hi, half + 1)
                    dve.tensor_tensor(y0lo[:, hs, :], G[:, hs, :], y0hi[:, hs, :].bitcast(F32), ALU.subtract)\
                       .then_inc(yc_ready, 1)
                if n in XBC:
                    conv(n, 4 + XBC.index(n), "ssd_conv_w", 2 * XBC_PAIR[n], XT, 12)
                if n - 1 in XBC:
                    i = XBC.index(n - 1)
                    p = XBC_PAIR[n - 1]
                    dve.wait_ge(xbc_th, i + 1)
                    xp = XT[:, 2 * p:2 * p + 2, :]
                    dve.scalar_tensor_tensor(xp, th[:, :, :], 1.0, xp, ALU.add, ALU.mult).then_inc(xbc_ready, 1)
                if n in XTR_AT:
                    p = XTR_AT.index(n)
                    if p == 0:
                        dve.wait_ge(tok_ready, 1)
                        dve.wait_ge(lru_scan, 2)
                    dve.wait_ge(x_tr, p + 1)
                    for c in range(2):
                        o = 2 * P * p + P * c
                        h0 = 32 + 4 * p + 2 * c
                        dt = tokm[:, 0:96].rearrange("p (j k) -> p j k", j=2)[:, :, h0:h0 + 2]
                        dve.tensor_tensor(XDM[:, :, o:o + P].rearrange("p j (h x) -> p j h x", h=2),
                                          banks[:, 4, 2 * P * c:2 * P * (c + 1)]
                                          .rearrange("p (j h x) -> p j h x", j=2, h=2),
                                          dt.unsqueeze(3).broadcast_to([P, 2, 2, DH]), ALU.mult)
                    dve.tensor_tensor(XDA[:, 2 * P * p:2 * P * (p + 1)].rearrange("p (h x) -> p h x", h=4),
                                      banks[0:META, 5, 0:2 * P].rearrange("p (h x) -> p h x", h=4),
                                      toka[:, 32 + 4 * p:36 + 4 * p].unsqueeze(2).broadcast_to([META, 4, DH]),
                                      ALU.mult).then_inc(xdt_done, 1)
                if n == CB_AT:
                    dve.wait_ge(cb_done, 1)
                    dve.wait_ge(lru_scan, 1)
                    dve.tensor_tensor(EA, banks[0:META, 5, TQ:2 * TQ].rearrange("p (h t) -> p h t", h=H),
                                      toka[:, 80:96].unsqueeze(2).broadcast_to([META, H, META]), ALU.add)\
                       .then_inc(ea_sum, 1)
                if n == CB_AT + 2:
                    dve.wait_ge(ea_exp, 1)
                    for g in range(2):
                        ins = dve.tensor_tensor(EA[:, 8 * g:8 * g + 8, :], EA[:, 8 * g:8 * g + 8, :],
                                                CBA[:, g, :].unsqueeze(1).broadcast_to([META, 8, META]), ALU.mult)
                    ins.then_inc(ea_done, 1)
                if SS <= n < SS + 8:
                    i = n - SS
                    g = i // 4
                    if i == 0:
                        dve.wait_ge(cb_done, 1)
                    for b in range(2):
                        dve.wait_ge(dec_exp, 2 * i + b + 1)
                        dve.tensor_tensor(E[:, b, :], E[:, b, :], CB[:, g, :], ALU.mult).then_inc(w_done, 1)
                if SS + 1 <= n < SS + 9:
                    c = n - SS - 1
                    dve.wait_ge(y_done, c + 1)
                    own.did(dve.scalar_tensor_tensor(ytmp, XT[:, c, OUTS], dcol[:, c:c + 1], banks[:, 6, 0:TQ],
                                                     ALU.mult, ALU.add))
                    own.settle()
                    dve.tensor_tensor(Z[:, c, :], Z[:, c, :], ytmp, ALU.mult).then_inc(y_evac, 1)
                if n in (SS + 6, SS + 10):
                    g = (n - SS - 6) // 4
                    dve.wait_ge(yb_hi, g + 1)
                    dve.tensor_tensor(y1lo[:, 4 * g:4 * g + 4, :], Z[:, 4 * g:4 * g + 4, :],
                                      y1hi[:, 4 * g:4 * g + 4, :].bitcast(F32), ALU.subtract).then_inc(yb_ready, 1)
                if n in (SS + 5, SS + 9):
                    g = (n - SS - 5) // 4
                    dve.wait_ge(grs_done, g + 1)
                    for c in range(4 * g, 4 * g + 4):
                        ins = dve.scalar_tensor_tensor(Z[:, c, :], Z[:, c, :], col("ssd_norm", c), acc[:, 0:TQ],
                                                       ALU.mult, ALU.mult)
                    ins.then_inc(yb_scaled, 1)
                if VV <= n < MG:
                    i = n - VV
                    dve.wait_ge(v_tr, i + 1)
                    dve.tensor_copy(VA[:, 2 * P * i:2 * P * (i + 1)], banks[0:META, 5, 0:2 * P]).then_inc(v_meta, 1)
                if VV + 2 <= n < VV + 19:
                    h = n - VV - 2
                    if h < H:
                        dve.wait_ge(s_mm, h + 1)
                        dve.reduce_max(NM[:, 2 * h:2 * h + 1], banks[:, 6, 0:144], AX_X, negate=True)
                        dve.reduce_max(NM[:, 2 * h + 1:2 * h + 2], banks[:, 6, 144:416], AX_X, negate=True)\
                           .then_inc(s_max, 1)
                    if h >= 1:
                        dve.wait_ge(p_tr, h)
                        if h >= 3:
                            dve.wait_ge(av_mm, h - 2)
                        dve.tensor_copy(PTA[:, (h - 1) % 2, :], banks[0:META, 5, 0:2 * P]).then_inc(pt_meta, 1)
                    if h < H:
                        dve.wait_ge(s_exp, h + 1)
                        own.did(dve.reciprocal(RI[:, 2 * h:2 * h + 2], RS[:, 2 * h:2 * h + 2]))
                        own.settle()
                        pr = PR[:, h % 2, :]
                        dve.tensor_scalar(pr[:, 0:144], pr[:, 0:144], RI[:, 2 * h:2 * h + 1], None, ALU.mult)
                        dve.tensor_scalar(pr[:, 144:416], pr[:, 144:416], RI[:, 2 * h + 1:2 * h + 2], None, ALU.mult)\
                           .then_inc(p_norm, 1)
                if n >= VV + 7 and (n - VV - 7) % 4 == 0 and (n - VV - 7) // 4 < 4:
                    g = (n - VV - 7) // 4
                    dve.wait_ge(av_mm, 4 * g + 4)
                    dve.tensor_copy(YA[:, 2 * g:2 * g + 2, :], banks[:, 4, :].rearrange("p (c t) -> p c t", c=2))\
                       .then_inc(ya_copied, 1)
                if n in YT_AT:
                    attn_lo(dve, YT_AT[n])
                if MG + 16 <= n < WO:
                    m = n - MG - 16
                    dve.wait_ge(mix_hi, m + 1)
                    dve.scalar_tensor_tensor(y1lo[:, m, :], MIX[:, m, :], 0.5, y1hi[:, m, :].bitcast(F32),
                                             ALU.mult, ALU.subtract).then_inc(mix_ready, 1)

                if n < GU2 - 2:
                    split_at(n + RING)

            split_at(GU2 + 1)
            norm(2, "ffn2_norm", OUTS)
            split_at(GU2 + 2)
            ffn(3, GU2, OUTS, FC)
            norm(3, "final_norm", OUTS)
            c, e = OUT_PARTS[-1]
            dve.wait_ge(o_tr, e)
            dve.tensor_copy(tokio[:, 0, P * c:P * e], banks[:, 2 * len(OUT_PARTS) - 2, 0:P * (e - c)]).then_inc(o_dve, 1)

        @block.tensor
        def _(pe):
            def product(bank_out, slot, kcs, tile, rhs, cols, start, stop, ya_pairs=None):
                for k in range(kcs):
                    if ya_pairs is not None:
                        pe.wait_ge(ya_ready, ya_pairs(k))
                    o = (2 * k + tile) * P
                    for i, (w, x) in enumerate(((whi, 0), (whi, 1), (wlo, 0))):
                        last = pe.matmul(bank_out, w[:, slot, o:o + P], rhs[x][:, rhs[2] + k, cols],
                                         start=start and k == 0 and i == 0, stop=stop and k == kcs - 1 and i == 2)
                return last

            def pair(n, slot, bank, rhs, cols, hi_ready, lo_ready, done):
                w = cols.stop - cols.start
                for k in range(KC):
                    for part, split in ((0, hi_ready), (1, lo_ready)):
                        pe.wait_ge(split, done + k + 1)
                        for t in range(2):
                            o = (2 * k + t) * P
                            for wt in ((whi, wlo) if part == 0 else (whi,)):
                                last = pe.matmul(banks[:, bank + t, 0:w], wt[:, slot, o:o + P], rhs[part][:, k, cols],
                                                 start=k == 0 and part == 0 and wt is whi,
                                                 stop=k == KC - 1 and part == 1)
                            if k == KC - 1 and part == 1:
                                last.then_inc(tiles_done, 1)

            def warm(bank):
                for _ in range(WARM):
                    pe.matmul(banks[:, bank, 0:P], ones[:, :], ones[:, :], start=True, stop=True)

            def stats(q, cols):
                w = cols.stop - cols.start
                if q > 0:
                    pe.wait_ge(sq_sum, q)
                    pe.matmul(banks[:, 7, 0:w], ones[:, :], acc[:, cols], start=True, stop=False)
                for c in range(C - 2 if q > 0 else 0, C):
                    pe.wait_ge(sq_done, 4 * q + c // 2 + 1)
                    last = pe.matmul(banks[:, 7, 0:w], ones[:, :], sq[:, c, cols], start=c == 0, stop=c == C - 1)
                last.then_inc(stat_done, 1)

            NRM = (thi, tlo, 0)
            Y0 = (y0hi, y0lo, 0)
            Y1 = (y1hi, y1lo, 0)

            pe.wait_ge(consts, 5)
            for _ in range(2):
                warm(7)
            pe.wait_ge(x_in, 32)
            for c in range(C):
                if c >= 6:
                    pe.wait_ge(x_new, c - 5)
                pe.transpose(banks[:, c % 6, 0:META], metain[:, P * c:P * (c + 1)], ident[0:META, 0:META])
                for j in range(2):
                    last = pe.transpose(banks[:, c % 6, META + P * j:META + P * (j + 1)],
                                        tokio[:, j, P * c:P * (c + 1)], ident[:, :])
                last.then_inc(xt_done, 1)
            stats(0, ALL)
            pe.wait_ge(vec_in, 16 * 12)
            pe.transpose(banks[:, 6, 0:nA], rows[0:nA, 0, :], ident[0:nA, 0:nA])
            pe.transpose(banks[:, 6, P:P + nB], rows[0:nB, 1, :], ident[0:nB, 0:nB]).then_inc(vt_done, 1)
            warm(5)

            def ffn(q, first, cols, base):
                w = cols.stop - cols.start

                def gate_up(n, slot, arr, turn, j, ready=None):
                    pe.wait_ge(lo_done, n + 1)
                    if base > 0 or not (isinstance(n, int) and n < first + RING):
                        pe.wait_ge(h_done, n + (base - first - RING + 1))
                    if ready is not None:
                        pair(n, slot, 2 * slot, NRM, cols, nhi_done, act_ready, ready)
                        return
                    for t in range(2):
                        product(banks[:, 2 * slot + t, 0:w], slot, KC, t, NRM, cols, True, True)\
                            .then_inc(tiles_done, 1)

                peel = RING if base == 0 else 1
                for n in range(first, first + peel):
                    gate_up(n, n % RING, 0, 0, 0, C * (q - 1) if n == first else None)
                rounds(pe, first + peel, FC - peel, gate_up)

                d0 = first + FC

                def down(n, slot, arr, turn, j):
                    kcs = FC - 16 if j == 2 else KC
                    pe.wait_ge(lo_done, n + 1)
                    if isinstance(n, int) and n < d0 + RING:
                        pe.wait_ge(hlo_done, base + 8 * j + kcs)
                        pe.wait_ge(h_done, base + FC - 2)
                    for t in range(2):
                        if j == 0 and not (isinstance(n, int) and n < d0 + RING):
                            pe.wait_ge(x_new, turn * 2 + (C * q + 1 + t))
                        product(banks[:, 2 + t, 0:w], slot, kcs, t, (hid_hi, hid_lo, 8 * j), cols,
                                j == 0, j == 2).then_inc(tiles_done, 1)

                for j in range(RING):
                    down(d0 + j, (d0 + j) % RING, 0, 0, j)
                rounds(pe, d0 + RING, 9, down)
                stats(q, cols)
                if q < 3:
                    warm(6)

            ffn(1, GU1, ALL, 0)

            def head(h):
                return slice(DH * (h % 2), DH * (h % 2) + DH), h // 2

            for n in range(FIRST, GU2):
                slot = n % RING
                pe.wait_ge(lo_done, n + 1)
                if FIRST + 2 <= n < WO + 2:
                    pe.wait_ge(evac[n % 2], freed(n - 2))
                elif n >= WO + 2:
                    pe.wait_ge(x_new, 2 * C + 2 * (n - WO - 2) + 2)
                cols = OUTS if n in GATE or n in ZZ or QQ <= n < VV or n >= MG else ALL
                w = cols.stop - cols.start
                if n == FIRST:
                    pair(n, slot, pj(n), NRM, cols, nhi_done, act_ready, C)
                elif n == FDT:
                    product(banks[:, pj(n), 0:w], slot, KC, 0, NRM, cols, True, True).then_inc(tiles_done, 2)
                elif n < MG:
                    for t in range(2):
                        product(banks[:, pj(n) + t, 0:w], slot, KC, t, NRM, cols, True, True)\
                            .then_inc(tiles_done, 1)
                elif n < WO:
                    product(banks[:, pj(n), 0:w], slot, KC, 0, NRM, cols, True, True).then_inc(tiles_done, 1)
                    k = n - MG
                    if k == 0:
                        pe.wait_ge(yc_ready, 2)
                    if k == C:
                        pe.wait_ge(yb_ready, 2)
                    product(banks[:, pj(n) + 1, 0:w], slot, KC, 1, Y1 if C <= k < 2 * C else Y0, slice(0, TQ),
                            True, True, (lambda c: c // 2 + 1) if k == 2 * C else None).then_inc(tiles_done, 1)
                elif n == WO:
                    pair(n, slot, pj(n), Y1, slice(0, TQ), mix_hi, mix_ready, 0)
                else:
                    for t in range(2):
                        product(banks[:, pj(n) + t, 0:w], slot, KC, t, Y1, slice(0, TQ), True, True)\
                            .then_inc(tiles_done, 1)

                if n == TOK_AT:
                    pe.wait_ge(fdt_dve, 2)
                    pe.wait_ge(lru_acted, 4)
                    for src, o, oa in ((sp48, 0, 192), (cs48, 96, 240)):
                        for j, ts in enumerate((S0, S1)):
                            pe.transpose(banks[:, 7, o + 48 * j:o + 48 * (j + 1)], src[:, ts], ident[0:48, 0:48])
                        last = pe.transpose(banks[0:META, 7, oa:oa + 48], src[:, S2], ident[0:48, 0:48])
                    last.then_inc(fdt_tr, 1)
                if n in LRU_AT:
                    i = LRU_AT.index(n)
                    pe.wait_ge(conv_done, i + 1)
                    if i == 0:
                        pe.wait_ge(lru_w_in, 64)
                    else:
                        pe.wait_ge(lru_acted, i)
                    for t in range(2):
                        c = 2 * i + t
                        pe.matmul(banks[:, 4 + 2 * t, 0:T], bda[:, c, :], XC[:, c, :], start=True, stop=True)
                        last = pe.matmul(banks[:, 5 + 2 * t, 0:T], bdx[:, c, :], XC[:, c, :], start=True, stop=True)
                    last.then_inc(lru_mm, 1)
                if n in XTR_AT:
                    p = XTR_AT.index(n)
                    pe.wait_ge(xbc_ready, p + 3)
                    if p == 0:
                        pe.wait_ge(cb_done, 1)
                        pe.wait_ge(ea_sum, 1)
                    else:
                        pe.wait_ge(xdt_done, p)
                    last = to_tokens(pe, lambda c, ts: XT[:, 2 * p + c, ts], (S0, S1), S2)
                    last.then_inc(x_tr, 1)
                if n == CB_AT:
                    pe.wait_ge(xbc_ready, 2)
                    pe.wait_ge(lru_acted, 4)
                    pe.wait_ge(tok_ready, 1)
                    for g in range(2):
                        B, Cm = XT[:, 8 + g, :], XT[:, 10 + g, :]
                        pe.matmul(banks[:, 4 + 2 * g, 0:TQ], B[:, S0], Cm[:, OUTS], start=True, stop=True)
                        pe.matmul(banks[:, 4 + 2 * g, TQ:W01], B[:, S1], Cm[:, P:T], start=True, stop=True)
                        last = pe.matmul(banks[0:META, 5 + 2 * g, 0:META], B[:, S2], Cm[:, S2], start=True, stop=True)
                    pe.wait_ge(cs_split, 1)
                    pe.matmul(banks[0:META, 5, TQ:2 * TQ], ones[32:48, 0:META], ablk, start=True, stop=False)
                    last = pe.matmul(banks[0:META, 5, TQ:2 * TQ].rearrange("p (h t) -> p h t", h=H),
                                     identb[:, 0:META], mask_st[:, 0:META].unsqueeze(1).broadcast_to([P, H, META]),
                                     start=False, stop=True)
                    last.then_inc(cb_mm, 1)
                if SS <= n < SS + 8:
                    i = n - SS
                    if i == 0:
                        pe.wait_ge(xdt_done, 4)
                        pe.wait_ge(sel_done, 1)
                    else:
                        pe.wait_ge(dec_exp, 2 * i)
                    for b in range(2):
                        h = 2 * i + b
                        row = 32 + h
                        for part in (cs_hi, cs_lo):
                            for o, e, ts in ((0, TQ, OUTS), (TQ, W01, slice(P, T))):
                                pe.matmul(banks[:, 4 + b, o:e], sel[32:48, row:row + 1].broadcast_to([H, P]),
                                          part[32:48, ts], start=part is cs_hi and o == 0, stop=False)
                        pe.matmul(banks[:, 4 + b, 0:P], identb[:, :], mask_s0[:, :], start=False, stop=False)
                        pe.matmul(banks[:, 4 + b, TQ:TQ + P], identb[:, :], mask_st[:, :], start=False, stop=True)\
                          .then_inc(dec_mm, 1)
                if SS + 1 <= n < SS + 9:
                    i = n - SS - 1
                    pe.wait_ge(w_done, 2 * i + 2)
                    if i == 0:
                        pe.wait_ge(ea_done, 1)
                    if i > 0:
                        pe.wait_ge(y_evac, i)
                    for b in range(2):
                        h = 2 * i + b
                        hs = slice(DH * h, DH * (h + 1))
                        y = banks[DH * b:DH * (b + 1), 6, :]
                        pe.matmul(y[:, 0:TQ], XDM[:, 0, hs], E[:, b, 0:TQ], start=True, stop=False)
                        pe.matmul(y[:, TQ - W1:TQ], XDM[:, 1, hs], E[:, b, TQ:W01], start=False, stop=False)
                        last = pe.matmul(y[:, TQ - META:TQ], XDA[:, hs], EA[:, h, :], start=False, stop=True)
                    last.then_inc(y_done, 1)
                if SS + 2 <= n < SS + 10:
                    c = n - SS - 2
                    pe.wait_ge(ysq_done, c + 1)
                    if c == 4:
                        pe.wait_ge(grs_done, 1)
                    pe.matmul(banks[:, 7, 0:TQ], ones[:, :], ysq, start=c % 4 == 0, stop=c % 4 == 3)\
                      .then_inc(gstat, 1)
                if VV + 2 <= n < VV + 20:
                    h = n - VV - 2
                    if h < H:
                        ps, c = head(h)
                        if h == 0:
                            pe.wait_ge(y_evac, C)
                        else:
                            pe.wait_ge(s_exp, h)
                        for o, e, q0, d in ((0, 144, 0, 16), (144, T, P, 288)):
                            s = banks[:, 6, o:o + e]
                            pe.matmul(s, QT[ps, c, q0:q0 + P], KT[ps, c, 0:e], start=o == 0, stop=False)
                            for part in (cs_hi, cs_lo):
                                pe.matmul(s, sel[0:H, h:h + 1].broadcast_to([H, P]), part[0:H, 0:e], start=False, stop=False)
                            last = pe.matmul(banks[:, 6, d:d + P], identb[:, :], mask_qk[:, :], start=False,
                                             stop=o > 0)
                        last.then_inc(s_mm, 1)
                if VV <= n < MG:
                    i = n - VV
                    pe.wait_ge(evac[n % 2], freed(n))
                    if i == 0:
                        pe.wait_ge(dec_exp, H)
                    else:
                        pe.wait_ge(v_main, i)
                        pe.wait_ge(v_meta, i)
                    to_tokens(pe, lambda c, ts: th[:, c, ts], (T0, T1), slice(0, META)).then_inc(v_tr, 1)
                if VV + 2 <= n < VV + 20:
                    if h >= 2:
                        attn_values(pe, h - 2)
                    if 1 <= h <= H:
                        k = h - 1
                        pe.wait_ge(p_norm, h)
                        if k == 0:
                            pe.wait_ge(grs_done, 2)
                            pe.wait_ge(v_meta, 4)
                        else:
                            pe.wait_ge(pt_main, k)
                            pe.wait_ge(pt_meta, k)
                        pr = PR[:, k % 2, :]
                        pe.transpose(banks[0:META, 5, 0:P], pr[:, 0:16], ident[:, :])
                        pe.transpose(banks[0:META, 5, P:2 * P], pr[:, 144:160], ident[:, :])
                        pe.transpose(banks[:, 7, 0:P], pr[:, 16:144], ident[:, :])
                        pe.transpose(banks[:, 7, P:2 * P], pr[:, 160:288], ident[:, :])
                        pe.transpose(banks[:, 7, 2 * P:3 * P], pr[:, 288:416], ident[:, :]).then_inc(p_tr, 1)

            stats(2, OUTS)
            warm(6)
            ffn(3, GU2, OUTS, FC)
            for c in range(C):
                pe.wait_ge(hn_done, 3 * C + c + 1)
                i, first = next((i, o) for i, (o, e) in enumerate(OUT_PARTS) if c < e)
                for j in range(2):
                    last = pe.transpose(banks[:, 2 * i + j, P * (c - first):P * (c - first + 1)],
                                        hn[:, c % RING, P * j:P * (j + 1)], ident[:, :])
                last.then_inc(o_tr, 1)


_OUT = "out_dram"


def kernel(**inputs):
    import numpy as _np
    import concourse.bacc as _bacc
    from concourse import mybir as _mybir
    from concourse.bass_utils import run_bass_kernel_spmd as _run

    nc = _bacc.Bacc("TRN2", target_bir_lowering=False, num_devices=1)
    arrays, aps = {}, {}
    for name, value in inputs.items():
        v = _np.ascontiguousarray(value)
        arrays[f"in_{name}"] = v
        aps[name] = nc.dram_tensor(f"in_{name}", v.shape, _mybir.dt.from_np(v.dtype), kind="ExternalInput").ap()
    shape = tuple(inputs["x"].shape)
    out = nc.dram_tensor(_OUT, shape, _mybir.dt.float32, kind="ExternalOutput").ap()
    hybrid_trunk(nc, aps, out)
    r = _run(nc, [arrays], core_ids=[0])
    return r.results[0][_OUT]
```
